# Optimizing a Trainium2 kernel written in Bass

```python
import jax, jax.numpy as jnp
from jax import lax
import numpy as np

D_MODEL = 1024
BATCH = 1
SEQ = 512
DEPTH = 2

HEAD_DIM = 64
Q_BLOCK = 128
ROPE_THETA = 10000.0
NORM_EPS = 1e-6
FOX_HEADS = 6
FOX_WIDTH = FOX_HEADS * HEAD_DIM
FORGET_BIAS_LO = 1.0
FORGET_BIAS_HI = 4.0
DIL_HEADS = 6
DIL_WIDTH = DIL_HEADS * HEAD_DIM
DIL_PAIRS = ((128, 1), (512, 4), (2048, 16))
DIL_BLOCK = 128
MLA_HEADS = 4
MLA_Q_RANK = 256
MLA_KV_RANK = 256
MLA_NOPE_DIM = 64
MLA_ROPE_DIM = 32
MLA_V_DIM = 64
MLA_WIDTH = MLA_HEADS * MLA_V_DIM
N_BRANCHES = 3
IN_SIZES = (FOX_WIDTH, FOX_WIDTH, FOX_WIDTH, FOX_HEADS,
            DIL_WIDTH, DIL_WIDTH, DIL_WIDTH,
            MLA_Q_RANK, MLA_KV_RANK, MLA_ROPE_DIM,
            N_BRANCHES * D_MODEL)
IN_WIDTH = sum(IN_SIZES)
D_FF = 2816
N_EXPERTS = 8
TOP_K = 2
D_FF_EXPERT = 1408
N_DENSE = (DEPTH + 1) // 2
N_MOE = DEPTH // 2
PLE_DIM = 256
MAX_POS_OFFSET = 1024

kernel_name = "hybrid_fox_dilated_mla_moe_trunk"

def rmsnorm(x, gain):
    xf = x.astype(jnp.float32)
    y = xf * lax.rsqrt(jnp.mean(xf * xf, axis=-1, keepdims=True) + NORM_EPS)
    return (y * gain.astype(jnp.float32)).astype(x.dtype)

def rope(x, positions):
    half = x.shape[-1] // 2
    inv_freq = ROPE_THETA ** (-jnp.arange(half, dtype=jnp.float32) / half)
    ang = positions.astype(jnp.float32)[:, None, :, None] * inv_freq
    cos, sin = jnp.cos(ang), jnp.sin(ang)
    xf = x.astype(jnp.float32)
    x1, x2 = xf[..., :half], xf[..., half:]
    return jnp.concatenate([x1 * cos - x2 * sin, x2 * cos + x1 * sin], axis=-1).astype(x.dtype)

def to_heads(a, n_heads):
    b, t, _ = a.shape
    return a.reshape(b, t, n_heads, -1).transpose(0, 2, 1, 3)

def from_heads(a):
    b, h, t, d = a.shape
    return a.transpose(0, 2, 1, 3).reshape(b, t, h * d)

def causal_block_attention(q, k, v, scale, decay=None):
    b, h, t, dk = q.shape
    nb = t // Q_BLOCK
    qb = q.reshape(b, h, nb, Q_BLOCK, dk).transpose(2, 0, 1, 3, 4)
    starts = jnp.arange(nb, dtype=jnp.int32) * Q_BLOCK
    k_pos = jnp.arange(t, dtype=jnp.int32)
    if decay is None:
        xs = (qb, starts)
    else:
        xs = (qb, starts, decay.reshape(b, h, nb, Q_BLOCK).transpose(2, 0, 1, 3))

    def one_block(xs_i):
        qi, start = xs_i[0], xs_i[1]
        s = jnp.einsum('bhqd,bhkd->bhqk', qi, k).astype(jnp.float32) * scale
        if decay is not None:
            s = s + (xs_i[2][..., :, None] - decay[:, :, None, :])
        q_pos = start + jnp.arange(Q_BLOCK, dtype=jnp.int32)
        s = jnp.where(k_pos[None, :] <= q_pos[:, None], s, -jnp.inf)
        pr = jax.nn.softmax(s, axis=-1)
        return jnp.einsum('bhqk,bhkd->bhqd', pr.astype(v.dtype), v)

    out = lax.map(one_block, xs)
    return out.transpose(1, 2, 0, 3, 4).reshape(b, h, t, v.shape[-1])

def dilated_branch(q, k, v, window, rate, scale):
    b, h, t, d = q.shape
    span = window // rate
    chunk = rate * DIL_BLOCK
    t_pad = -(-t // chunk) * chunk
    length = t_pad // rate
    nb = length // DIL_BLOCK

    def blocks(a):
        a = jnp.pad(a, ((0, 0), (0, 0), (0, t_pad - t), (0, 0)))
        a = a.reshape(b, h, length, rate, d).transpose(0, 1, 3, 2, 4)
        return a.reshape(b, h, rate, nb, DIL_BLOCK, d)

    def with_prev(a):
        prev = jnp.concatenate([jnp.zeros_like(a[:, :, :, :1]), a[:, :, :, :-1]], axis=3)
        return jnp.concatenate([prev, a], axis=4)

    qb = blocks(q)
    kb = with_prev(blocks(k))
    vb = with_prev(blocks(v))
    s = jnp.einsum('bhrnqd,bhrnkd->bhrnqk', qb, kb).astype(jnp.float32) * scale
    qi = jnp.arange(DIL_BLOCK)[:, None]
    ki = jnp.arange(2 * DIL_BLOCK)[None, :]
    dist = qi + DIL_BLOCK - ki
    band = (dist >= 0) & (dist <= span)
    has_prev = (jnp.arange(nb) > 0)[:, None, None] | (ki >= DIL_BLOCK)[None]
    valid = band[None] & has_prev
    s = jnp.where(valid, s, -jnp.inf)
    lse = jax.nn.logsumexp(s, axis=-1)
    pr = jnp.exp(s - lse[..., None])
    o = jnp.einsum('bhrnqk,bhrnkd->bhrnqd', pr.astype(v.dtype), vb)
    o = o.reshape(b, h, rate, length, d).transpose(0, 1, 3, 2, 4).reshape(b, h, t_pad, d)[:, :, :t]
    lse = lse.reshape(b, h, rate, length).transpose(0, 1, 3, 2).reshape(b, h, t_pad)[:, :, :t]
    return o, lse

def dilated_attention(q, k, v, scale):
    results = [dilated_branch(q, k, v, w, r, scale) for (w, r) in DIL_PAIRS]
    outs = jnp.stack([o for o, _ in results], axis=0)
    lses = jnp.stack([l for _, l in results], axis=0)
    alpha = jax.nn.softmax(lses, axis=0)
    return jnp.einsum('gbht,gbhtd->bhtd', alpha.astype(v.dtype), outs)

def swiglu(h, w_gate, w_up, w_down):
    return (jax.nn.silu(h @ w_gate) * (h @ w_up)) @ w_down

def moe_swiglu(h, w_router, w_gate, w_up, w_down):
    logits = (h @ w_router).astype(jnp.float32)
    top_val, top_idx = lax.top_k(logits, TOP_K)
    top_w = jax.nn.softmax(top_val, axis=-1)
    combine = jnp.sum(jax.nn.one_hot(top_idx, N_EXPERTS, dtype=jnp.float32) * top_w[..., None], axis=-2)
    combine = combine.astype(h.dtype)
    y = jnp.zeros_like(h)
    for e in range(N_EXPERTS):
        y = y + combine[..., e:e + 1] * swiglu(h, w_gate[e], w_up[e], w_down[e])
    return y

def setup_inputs(seed: int = 0) -> dict:
    key = jax.random.key(seed)
    ks = iter(jax.random.split(key, 32))
    f32 = jnp.float32

    def normal(shape, fan_in):
        return jax.random.normal(next(ks), shape, f32) * (fan_in ** -0.5)

    def gain(shape):
        return 1.0 + 0.05 * jax.random.normal(next(ks), shape, f32)

    x = jax.random.normal(next(ks), (BATCH, SEQ, D_MODEL), f32)
    p = jax.random.normal(next(ks), (DEPTH, BATCH, SEQ, PLE_DIM), f32)
    offsets = jax.random.randint(next(ks), (BATCH, 1), 0, MAX_POS_OFFSET, dtype=jnp.int32)
    positions = offsets + jnp.arange(SEQ, dtype=jnp.int32)[None, :]
    return {
        'x': x,
        'p': p,
        'positions': positions,
        'mix_norm': gain((DEPTH, D_MODEL)),
        'w_in': normal((DEPTH, D_MODEL, IN_WIDTH), D_MODEL),
        'b_forget': jax.random.uniform(next(ks), (DEPTH, FOX_HEADS), f32, FORGET_BIAS_LO, FORGET_BIAS_HI),
        'mla_q_norm': gain((DEPTH, MLA_Q_RANK)),
        'mla_kv_norm': gain((DEPTH, MLA_KV_RANK)),
        'w_uq': normal((DEPTH, MLA_Q_RANK, MLA_HEADS * (MLA_NOPE_DIM + MLA_ROPE_DIM)), MLA_Q_RANK),
        'w_ukv': normal((DEPTH, MLA_KV_RANK, MLA_HEADS * (MLA_NOPE_DIM + MLA_V_DIM)), MLA_KV_RANK),
        'w_br_fox': normal((DEPTH, FOX_WIDTH, D_MODEL), FOX_WIDTH),
        'w_br_dil': normal((DEPTH, DIL_WIDTH, D_MODEL), DIL_WIDTH),
        'w_br_mla': normal((DEPTH, MLA_WIDTH, D_MODEL), MLA_WIDTH),
        'w_out': normal((DEPTH, D_MODEL, D_MODEL), D_MODEL),
        'ffn_norm': gain((DEPTH, D_MODEL)),
        'w_ffn_gate': normal((N_DENSE, D_MODEL, D_FF), D_MODEL),
        'w_ffn_up': normal((N_DENSE, D_MODEL, D_FF), D_MODEL),
        'w_ffn_down': normal((N_DENSE, D_FF, D_MODEL), D_FF),
        'w_router': normal((N_MOE, D_MODEL, N_EXPERTS), D_MODEL),
        'w_exp_gate': normal((N_MOE, N_EXPERTS, D_MODEL, D_FF_EXPERT), D_MODEL),
        'w_exp_up': normal((N_MOE, N_EXPERTS, D_MODEL, D_FF_EXPERT), D_MODEL),
        'w_exp_down': normal((N_MOE, N_EXPERTS, D_FF_EXPERT, D_MODEL), D_FF_EXPERT),
        'ple_norm': gain((DEPTH, D_MODEL)),
        'w_ple_gate': normal((DEPTH, D_MODEL, D_MODEL), D_MODEL),
        'w_ple_proj': normal((DEPTH, PLE_DIM, D_MODEL), PLE_DIM),
        'final_norm': gain((D_MODEL,)),
    }

def reference(x, p, positions, mix_norm, w_in, b_forget, mla_q_norm, mla_kv_norm, w_uq, w_ukv,
              w_br_fox, w_br_dil, w_br_mla, w_out, ffn_norm, w_ffn_gate, w_ffn_up, w_ffn_down,
              w_router, w_exp_gate, w_exp_up, w_exp_down, ple_norm, w_ple_gate, w_ple_proj,
              final_norm):
    b, t, _ = x.shape
    split_at = np.cumsum(IN_SIZES)[:-1].tolist()
    head_scale = HEAD_DIM ** -0.5
    mla_scale = (MLA_NOPE_DIM + MLA_ROPE_DIM) ** -0.5
    for i in range(DEPTH):
        h = rmsnorm(x, mix_norm[i])
        proj = h @ w_in[i]
        (fq, fk, fv, fz, dq, dk, dv, cq, ckv, kr, gates) = jnp.split(proj, split_at, axis=-1)

        log_f = jax.nn.log_sigmoid(fz.astype(jnp.float32) + b_forget[i].astype(jnp.float32))
        decay = jnp.cumsum(log_f, axis=1).transpose(0, 2, 1)
        o_fox = causal_block_attention(to_heads(fq, FOX_HEADS), to_heads(fk, FOX_HEADS),
                                       to_heads(fv, FOX_HEADS), head_scale, decay)

        o_dil = dilated_attention(rope(to_heads(dq, DIL_HEADS), positions),
                                  rope(to_heads(dk, DIL_HEADS), positions),
                                  to_heads(dv, DIL_HEADS), head_scale)

        q_c = to_heads(rmsnorm(cq, mla_q_norm[i]) @ w_uq[i], MLA_HEADS)
        q_c = jnp.concatenate([q_c[..., :MLA_NOPE_DIM], rope(q_c[..., MLA_NOPE_DIM:], positions)], axis=-1)
        kv_c = to_heads(rmsnorm(ckv, mla_kv_norm[i]) @ w_ukv[i], MLA_HEADS)
        k_pe = rope(kr[:, None], positions)
        k_c = jnp.concatenate([kv_c[..., :MLA_NOPE_DIM],
                               jnp.broadcast_to(k_pe, (b, MLA_HEADS, t, MLA_ROPE_DIM))], axis=-1)
        o_mla = causal_block_attention(q_c, k_c, kv_c[..., MLA_NOPE_DIM:], mla_scale)

        g_fox, g_dil, g_mla = jnp.split(jax.nn.sigmoid(gates), N_BRANCHES, axis=-1)
        merged = (g_fox * (from_heads(o_fox) @ w_br_fox[i])
                  + g_dil * (from_heads(o_dil) @ w_br_dil[i])
                  + g_mla * (from_heads(o_mla) @ w_br_mla[i]))
        x = x + merged @ w_out[i]

        h = rmsnorm(x, ffn_norm[i])
        j = i // 2
        if i % 2 == 0:
            x = x + swiglu(h, w_ffn_gate[j], w_ffn_up[j], w_ffn_down[j])
        else:
            x = x + moe_swiglu(h, w_router[j], w_exp_gate[j], w_exp_up[j], w_exp_down[j])

        g = jax.nn.sigmoid(rmsnorm(x, ple_norm[i]) @ w_ple_gate[i])
        x = x + g * (p[i] @ w_ple_proj[i])
    return rmsnorm(x, final_norm)


_drawn_inputs = setup_inputs


def setup_inputs(seed=0):
    import zlib

    import numpy as np

    out = dict(_drawn_inputs(seed))
    spreads = {}
    factors = {'mla_q_norm': 3.361, 'mla_kv_norm': 3.019}
    for name, (base, spread) in spreads.items():
        noise = np.random.default_rng([zlib.crc32(name.encode()), seed]).standard_normal(out[name].shape)
        drawn = base * np.exp(spread * noise) if base else spread * noise
        out[name] = __import__('jax').numpy.asarray(drawn.astype(out[name].dtype))
    for name, factor in factors.items():
        out[name] = (out[name] * factor).astype(out[name].dtype)
    return out
```

```python
from contextlib import ExitStack, contextmanager

import numpy as np

import concourse.bass as bass
from concourse import mybir

F32 = mybir.dt.float32
F32R = mybir.dt.float32r
I32 = mybir.dt.int32
U32 = mybir.dt.uint32
ALU = mybir.AluOpType
ACT = mybir.ActivationFunctionType

P = 128
D = 1024
T = 512
DEPTH = 2
HD = 64
KC = D // P
TB = T // P
FOX_HEADS = DIL_HEADS = 6
MLA_HEADS = 4
NOPE, ROPE_M = 64, 32
QK_M = NOPE + ROPE_M
WIDTH = FOX_HEADS * HD
RANK = 256
PLE = 256
EXPERTS = 8
F_EXP = 1408
FB = F_EXP // P
UNIT_CHUNKS = FB
UNIT = UNIT_CHUNKS * P
EPS = 1e-6
THETA = 10000.0
MASKED = -1e30
CREDIT = 4

C_FQ, C_FK, C_FV = 0, WIDTH, 2 * WIDTH
C_FZ = 3 * WIDTH
C_DQ = C_FZ + FOX_HEADS
C_DK, C_DV = C_DQ + WIDTH, C_DQ + 2 * WIDTH
C_CQ = C_DQ + 3 * WIDTH
C_CKV = C_CQ + RANK
C_KR = C_CKV + RANK
C_GATES = C_KR + ROPE_M

K_IDENT, K_ONES, K_ROTD, K_ROTM = 0, P, 2 * P, 3 * P
K_BIAS = 4 * P
K_FREQ = K_BIAS + 2 * T
K_EPS, K_HALFPI = K_FREQ + 2, K_FREQ + 3
K_IOTA = K_FREQ + 4
K_COLS = K_IOTA + EXPERTS

EXPERT_UNITS = 2 * FB + KC
SETUP_LANDED = 16 * (2 + 5 * DEPTH + 3)

TWO_PI = 2 * np.pi
PI_A = 6.28125
PI_B = float(np.float32(np.round((TWO_PI - PI_A) * 2**21) / 2**21))
PI_C = float(np.float32(TWO_PI - PI_A - PI_B))
SIN_MAX = 3.1415925
ROUND_MAGIC = 1.5 * 2.0**23
DIL_PAIRS = ((128, 1), (512, 4), (2048, 16))


def constant_table():
    c = np.zeros((P, K_COLS), np.float32)
    c[:, K_IDENT:K_IDENT + P] = np.eye(P)
    c[:, K_ONES:K_ONES + P] = 1.0
    for base, width, half in ((0, HD, HD // 2), (HD, HD, HD // 2)):
        for i in range(half):
            c[base + i + half, K_ROTD + base + i] = -1.0
            c[base + i, K_ROTD + base + i + half] = 1.0
    for i in range(ROPE_M // 2):
        c[NOPE + i + ROPE_M // 2, K_ROTM + NOPE + i] = -1.0
        c[NOPE + i, K_ROTM + NOPE + i + ROPE_M // 2] = 1.0
    q = np.arange(P)[:, None]
    dist = q + (TB - 1) * P - np.arange(T)[None, :]
    c[:, K_BIAS:K_BIAS + T] = np.where(dist >= 0, 0.0, MASKED)
    times = sum(((dist >= 0) & (dist % r == 0) & (dist <= w)).astype(np.float64) for w, r in DIL_PAIRS)
    c[:, K_BIAS + T:K_BIAS + 2 * T] = np.where(times > 0, np.log(np.maximum(times, 1)), MASKED)
    half = HD // 2
    f = THETA ** (-(np.arange(half, dtype=np.float32) / half).astype(np.float64))
    c[:, K_FREQ] = np.tile(f, P // half)
    half = ROPE_M // 2
    f = THETA ** (-(np.arange(half, dtype=np.float32) / half).astype(np.float64))
    c[NOPE:NOPE + ROPE_M, K_FREQ + 1] = np.tile(f, 2)
    c[:, K_EPS] = EPS
    c[:, K_HALFPI] = np.pi / 2
    c[:, K_IOTA:K_IOTA + EXPERTS] = np.arange(EXPERTS)
    return c


class Tally:

    def __init__(self, sem, start=CREDIT):
        self.sem, self.base, self.k = sem, start, 0

    def add(self, n=1):
        self.k += n

    def inc(self):
        self.k += 1
        return 1

    def next(self, n=1):
        self.k += n
        return self.base + self.k

    def now(self, back=0):
        return self.base + (self.k - back)


class Tallies:

    def __init__(self, s):
        self.w_landed0 = Tally(s["w_landed0"], 0)
        self.w_landed1 = Tally(s["w_landed1"], 0)
        self.setup_landed = Tally(s["setup_landed"], 0)
        self.x_landed = Tally(s["x_landed"], 0)
        self.p_landed = Tally(s["p_landed"], 0)
        self.negd_landed = Tally(s["negd_landed"], 0)
        self.out_landed = Tally(s["out_landed"], 0)
        self.unit_done = Tally(s["unit_done"])
        self.x_turns = Tally(s["x_turns"])
        self.v_turns = Tally(s["v_turns"])
        self.p_turns = Tally(s["p_turns"])
        self.out_turns = Tally(s["out_turns"])
        self.norm_mm = Tally(s["norm_mm"])
        self.rot_done = Tally(s["rot_done"])
        self.s_done = Tally(s["s_done"])
        self.t_done = Tally(s["t_done"])
        self.pv_done = Tally(s["pv_done"])
        self.route_done = Tally(s["route_done"])
        self.hi_done = Tally(s["hi_done"])
        self.act_step = Tally(s["act_step"])
        self.sq_ready = Tally(s["sq_ready"])
        self.root_ready = Tally(s["root_ready"])
        self.hn_ready = Tally(s["hn_ready"])
        self.raw_ready = Tally(s["raw_ready"])
        self.k_ready = Tally(s["k_ready"])
        self.sig_ready = Tally(s["sig_ready"])
        self.mhi_ready = Tally(s["mhi_ready"])
        self.ahi_ready = Tally(s["ahi_ready"])
        self.exp_done = Tally(s["exp_done"])
        self.pt_even = Tally(s["pt_even"])
        self.ohi_ready = Tally(s["ohi_ready"])
        self.fz_ready = Tally(s["fz_ready"])
        self.phi_ready = Tally(s["phi_ready"])
        self.pp_ready = Tally(s["pp_ready"])
        self.share_ready = Tally(s["share_ready"])
        self.dve_step = Tally(s["dve_step"])
        self.raw_zeroed = Tally(s["raw_zeroed"])
        self.x_turned = Tally(s["x_turned"])
        self.ang_ready = Tally(s["ang_ready"])
        self.hf_ready = Tally(s["hf_ready"])
        self.hlo_ready = Tally(s["hlo_ready"])
        self.q_ready = Tally(s["q_ready"])
        self.rope_ready = Tally(s["rope_ready"])
        self.v_ready = Tally(s["v_ready"])
        self.fz_taken = Tally(s["fz_taken"])
        self.negd_ready = Tally(s["negd_ready"])
        self.s_taken = Tally(s["s_taken"])
        self.neg_ready = Tally(s["neg_ready"])
        self.p_ready = Tally(s["p_ready"])
        self.pt_odd = Tally(s["pt_odd"])
        self.olo_ready = Tally(s["olo_ready"])
        self.m_ready = Tally(s["m_ready"])
        self.mlo_ready = Tally(s["mlo_ready"])
        self.x_upd = Tally(s["x_upd"])
        self.af_ready = Tally(s["af_ready"])
        self.alo_ready = Tally(s["alo_ready"])
        self.plo_ready = Tally(s["plo_ready"])
        self.out_ready = Tally(s["out_ready"])
        self.xn_ready = Tally(s["xn_ready"])
        self.comb_ready = Tally(s["comb_ready"])
        self.wr_ready = Tally(s["wr_ready"])
        self.qrow_ready = Tally(s["qrow_ready"])
        self.gap_ready = Tally(s["gap_ready"])
        self.lo_done = Tally(s["lo_done"])
        self.staged = Tally(s["staged"])


@contextmanager
def turns(eng, count, per):
    with eng.Fori(0, count) as i:
        saved = {t: (t.base, t.k) for t in per}
        for t, n in per.items():
            t.base, t.k = t.now() + i * n, 0
        yield i
        for t, n in per.items():
            assert t.k == n, (t.sem, t.k, n)
    for t, n in per.items():
        t.base, t.k = saved[t][0], saved[t][1] + count * n


def build_trunk(nc, a, out):
    with ExitStack() as ctx:
        def sb(name, shape, dt=F32):
            return ctx.enter_context(nc.sbuf_tensor(name, shape, dt))

        x = sb("x", [P, KC, T])
        h_hi, h_lo = sb("h_hi", [P, KC, T], F32R), sb("h_lo", [P, KC, T], F32R)
        w_raw = sb("w_raw", [P, 2, UNIT])
        w_hi, w_lo = sb("w_hi", [P, 2, UNIT], F32R), sb("w_lo", [P, 2, UNIT], F32R)
        def slab(name, nbytes):
            start = -(-nc.sbuf_base // 32) * 32
            sb(name, [P, nbytes // 4 + 8])
            assert start + nbytes <= nc.sbuf_base
            return start

        at0, at1 = slab("slab0", 65536), slab("slab1", 16384)
        const = sb("const", [P, K_COLS])
        gains = sb("gains", [P, 3 * DEPTH + 1, KC])
        gains_r = sb("gains_r", [P, 2 * DEPTH, RANK // P])
        b_forget = sb("b_forget", [FOX_HEADS, DEPTH])
        cos_d, sin_d = sb("cos_d", [P, T]), sb("sin_d", [P, T])
        cos_m, sin_m = sb("cos_m", [P, T]), sb("sin_m", [P, T])
        tmp = sb("tmp", [P, 4, T])
        sq = sb("sq", [P, 2, T])
        rstd = sb("rstd", [P, T])
        pt = sb("pt", [P, 10 * P])
        q_st = sb("q_st", [P, 2, T])
        v_st = sb("v_st", [P, 2, TB, HD])
        smax, sneg = sb("smax", [P, 2, TB]), sb("sneg", [P, 2, TB])
        ssum, srec = sb("ssum", [P, 2, TB]), sb("srec", [P, 2, TB])
        gate = sb("gate", [P, 12])
        route = sb("route", [P, 12, TB, EXPERTS])
        route_i = sb("route_i", [P, TB, EXPERTS], U32)
        wr_raw = sb("wr_raw", [P, KC, EXPERTS])
        wr_hi, wr_lo = sb("wr_hi", [P, KC, EXPERTS], F32R), sb("wr_lo", [P, KC, EXPERTS], F32R)

        def at(name, shape, dt, offset):
            return nc.alloc_sbuf_tensor_at(name, shape, dt, offset=offset)

        o_hi = at("o_hi", [P, KC, T], F32R, at0)
        o_lo = at("o_lo", [P, KC, T], F32R, at0 + 16384)
        q_all = at("q_all", [P, FOX_HEADS, T], F32, at0 + 32768)
        k_all = at("k_all", [P, FOX_HEADS, T], F32, at0 + 45056)
        v_all = at("v_all", [P, TB, WIDTH], F32, at0 + 57344)
        probs = at("probs", [P, 2, TB, T], F32, at1)
        scan = at("scan", [FOX_HEADS, 2, T], F32, at1)
        scan_t = at("scan_t", [FOX_HEADS, 4, T], F32, at1 + 4096)
        cq_raw = at("cq_raw", [P, 2, T], F32, at1)
        cn_hi = at("cn_hi", [P, 2, T], F32R, at1 + 4096)
        cn_lo = at("cn_lo", [P, 2, T], F32R, at1 + 8192)
        ckv_raw = at("ckv_raw", [P, 2, T], F32, at1 + 12288)
        m_hi = at("m_hi", [P, KC, T], F32R, at0 + 32768)
        m_lo = at("m_lo", [P, KC, T], F32R, at0 + 49152)
        sg = at("sg", [P, 3, T], F32, at1)
        a_hi = at("a_hi", [P, FB, T], F32R, at0)
        a_lo = at("a_lo", [P, FB, T], F32R, at0 + 22528)
        p_hi = at("p_hi", [P, PLE // P, T], F32R, at0 + 45056)
        p_lo = at("p_lo", [P, PLE // P, T], F32R, at0 + 49152)
        comb_b = at("comb_b", [P, T], F32, at0 + 53248)
        comb_t = at("comb_t", [EXPERTS, 2, T], F32, at0 + 55296)
        p_tok = at("p_tok", [P, TB, PLE], F32, at1 + 8192)
        pp = at("pp", [P, KC, T], F32, at0)
        x_tok = at("x_tok", [P, TB, D], F32, at1)
        pos_i = at("pos_i", [P, T], I32, at0)
        trig = at("trig", [P, 4, T], F32, at0 + 2048)

        ident = const[:, K_IDENT:K_IDENT + P]
        ones = const[:, K_ONES:K_ONES + P]
        rot_d = const[:, K_ROTD:K_ROTD + P]
        rot_m = const[0:QK_M, K_ROTM:K_ROTM + QK_M]

        ps = ctx.enter_context(nc.psum_tensor("ps", [P, 8, T], F32))

        def sem(name):
            return ctx.enter_context(nc.semaphore(name))

        w_landed0 = sem("w_landed0")
        w_landed1 = sem("w_landed1")
        setup_landed = sem("setup_landed")
        x_landed = sem("x_landed")
        p_landed = sem("p_landed")
        negd_landed = sem("negd_landed")
        out_landed = sem("out_landed")
        unit_done = sem("unit_done")
        x_turns = sem("x_turns")
        v_turns = sem("v_turns")
        p_turns = sem("p_turns")
        out_turns = sem("out_turns")
        norm_mm = sem("norm_mm")
        rot_done = sem("rot_done")
        s_done = sem("s_done")
        t_done = sem("t_done")
        pv_done = sem("pv_done")
        route_done = sem("route_done")
        hi_done = sem("hi_done")
        act_step = sem("act_step")
        sq_ready = sem("sq_ready")
        root_ready = sem("root_ready")
        hn_ready = sem("hn_ready")
        raw_ready = sem("raw_ready")
        k_ready = sem("k_ready")
        sig_ready = sem("sig_ready")
        mhi_ready = sem("mhi_ready")
        ahi_ready = sem("ahi_ready")
        exp_done = sem("exp_done")
        pt_even = sem("pt_even")
        ohi_ready = sem("ohi_ready")
        fz_ready = sem("fz_ready")
        phi_ready = sem("phi_ready")
        pp_ready = sem("pp_ready")
        share_ready = sem("share_ready")
        dve_step = sem("dve_step")
        raw_zeroed = sem("raw_zeroed")
        x_turned = sem("x_turned")
        ang_ready = sem("ang_ready")
        hf_ready = sem("hf_ready")
        hlo_ready = sem("hlo_ready")
        q_ready = sem("q_ready")
        rope_ready = sem("rope_ready")
        v_ready = sem("v_ready")
        fz_taken = sem("fz_taken")
        negd_ready = sem("negd_ready")
        s_taken = sem("s_taken")
        neg_ready = sem("neg_ready")
        p_ready = sem("p_ready")
        pt_odd = sem("pt_odd")
        olo_ready = sem("olo_ready")
        m_ready = sem("m_ready")
        mlo_ready = sem("mlo_ready")
        x_upd = sem("x_upd")
        af_ready = sem("af_ready")
        alo_ready = sem("alo_ready")
        plo_ready = sem("plo_ready")
        out_ready = sem("out_ready")
        xn_ready = sem("xn_ready")
        comb_ready = sem("comb_ready")
        wr_ready = sem("wr_ready")
        qrow_ready = sem("qrow_ready")
        gap_ready = sem("gap_ready")
        lo_done = sem("lo_done")
        staged = sem("staged")
        sems = dict(
            w_landed0=w_landed0, w_landed1=w_landed1, setup_landed=setup_landed, x_landed=x_landed,
            p_landed=p_landed, negd_landed=negd_landed, out_landed=out_landed, unit_done=unit_done,
            x_turns=x_turns, v_turns=v_turns, p_turns=p_turns, out_turns=out_turns, norm_mm=norm_mm,
            rot_done=rot_done, s_done=s_done, t_done=t_done, pv_done=pv_done, route_done=route_done,
            hi_done=hi_done, act_step=act_step, sq_ready=sq_ready, root_ready=root_ready,
            hn_ready=hn_ready, raw_ready=raw_ready, k_ready=k_ready, sig_ready=sig_ready,
            mhi_ready=mhi_ready, ahi_ready=ahi_ready, exp_done=exp_done, pt_even=pt_even,
            ohi_ready=ohi_ready, fz_ready=fz_ready, phi_ready=phi_ready, pp_ready=pp_ready,
            share_ready=share_ready, dve_step=dve_step, raw_zeroed=raw_zeroed, x_turned=x_turned,
            ang_ready=ang_ready, hf_ready=hf_ready, hlo_ready=hlo_ready, q_ready=q_ready,
            rope_ready=rope_ready, v_ready=v_ready, fz_taken=fz_taken, negd_ready=negd_ready,
            s_taken=s_taken, neg_ready=neg_ready, p_ready=p_ready, pt_odd=pt_odd,
            olo_ready=olo_ready, m_ready=m_ready, mlo_ready=mlo_ready, x_upd=x_upd,
            af_ready=af_ready, alo_ready=alo_ready, plo_ready=plo_ready, out_ready=out_ready,
            xn_ready=xn_ready, comb_ready=comb_ready, wr_ready=wr_ready, qrow_ready=qrow_ready,
            gap_ready=gap_ready, lo_done=lo_done, staged=staged)

        def rows(w, chunks):
            return w.rearrange("(c p) n -> p c n", c=chunks)

        block = ctx.enter_context(nc.Block())

        @block.sync
        def _(sp):
            t = Tallies(sems)
            loads = Tally(lo_done)
            landed = [t.w_landed0, t.w_landed1]
            slot = [0]

            def load(src, chunks, width):
                s = slot[0]
                sp.wait_ge(lo_done, loads.now(back=1))
                dst = w_raw[:, s, 0:chunks * width].rearrange("p (c n) -> p c n", c=chunks)
                sp.dma_start(dst, src).then_inc(landed[s].sem, 16)
                loads.add()
                slot[0] = 1 - s

            def cols(w, chunks, c0, width=P):
                start = c0 if isinstance(c0, int) else sp.snap(c0)
                return rows(w, chunks)[:, :, bass.ds(start, width)]

            sp.dma_start(const[:], a["const"]).then_inc(setup_landed, 16)
            sp.dma_start(x_tok[:], a["x"][0].rearrange("(b p) d -> p b d", p=P)).then_inc(x_landed, 16)
            sp.dma_start(pos_i[:], a["positions"].to_broadcast([P, T])).then_inc(setup_landed, 16)
            with nc.allow_non_contiguous_dma(reason="small gain vectors"):
                for l in range(DEPTH):
                    for n, name in enumerate(("mix_norm", "ffn_norm", "ple_norm")):
                        sp.dma_start(gains[:, 3 * l + n, :], a[name][l].rearrange("(c p) -> p c", p=P)).then_inc(setup_landed, 16)
                    for n, name in enumerate(("mla_q_norm", "mla_kv_norm")):
                        sp.dma_start(gains_r[:, 2 * l + n, :], a[name][l].rearrange("(c p) -> p c", p=P)).then_inc(setup_landed, 16)
                sp.dma_start(gains[:, 3 * DEPTH, :], a["final_norm"].rearrange("(c p) -> p c", p=P)).then_inc(setup_landed, 16)
                sp.dma_start(b_forget[:], a["b_forget"].rearrange("l h -> h l")).then_inc(setup_landed, 16)

            sp.dma_start(wr_raw[:], a["w_router"][0].rearrange("(c p) n -> p c n", p=P)).then_inc(setup_landed, 16)
            sp.wait_ge(raw_zeroed, t.raw_zeroed.next())
            for l in range(DEPTH):
                w_in = a["w_in"][l]
                with turns(sp, 3, {loads: 2}) as j:
                    load(cols(w_in, KC, C_FQ + j * P), KC, P)
                    load(cols(w_in, KC, C_FK + j * P), KC, P)
                for j in range(3):
                    load(cols(w_in, KC, C_FV + j * P), KC, P)
                load(cols(w_in, KC, C_FZ), KC, P)
                with turns(sp, 3, {loads: 2}) as j:
                    load(cols(w_in, KC, C_DQ + j * P), KC, P)
                    load(cols(w_in, KC, C_DK + j * P), KC, P)
                for j in range(3):
                    load(cols(w_in, KC, C_DV + j * P), KC, P)
                for c in (C_CQ, C_CQ + P, C_CKV, C_CKV + P, C_KR - NOPE):
                    load(cols(w_in, KC, c), KC, P)
                load(rows(a["w_uq"][l], 2), 2, MLA_HEADS * QK_M)
                load(rows(a["w_ukv"][l], 2), 2, MLA_HEADS * P)
                with turns(sp, KC, {loads: 4}) as m:
                    for b in range(3):
                        load(cols(w_in, KC, C_GATES + b * D + m * P), KC, P)
                    s = slot[0]
                    branches = [(n, rows(a[name][l], n)[:, :, bass.ds(m * (P // 2) * 2, P)]) for name, n in (("w_br_fox", 3), ("w_br_dil", 3), ("w_br_mla", 2))]
                    sp.wait_ge(lo_done, loads.now(back=1))
                    at_chunk = 0
                    for n, src in branches:
                        dst = w_raw[:, s, at_chunk * P:(at_chunk + n) * P].rearrange("p (c n) -> p c n", c=n)
                        sp.dma_start(dst, src).then_inc(landed[s].sem, 16)
                        at_chunk += n
                    loads.add()
                    slot[0] = 1 - s
                with turns(sp, KC // 2, {loads: 2}) as m:
                    for s in range(2):
                        load(cols(a["w_out"][l], KC, m * 2 * P + s * P), KC, P)
                sp.dma_start(p_tok[:], a["p"][l, 0].rearrange("(b p) d -> p b d", p=P)).then_inc(p_landed, 16)

                def expert(gate_w, up_w, down_w, col0=0):
                    with turns(sp, FB, {loads: 2}) as f:
                        load(cols(gate_w, KC, col0 + f * P), KC, P)
                        load(cols(up_w, KC, col0 + f * P), KC, P)
                    with turns(sp, KC // 2, {loads: 2}) as m:
                        for s in range(2):
                            load(cols(down_w, FB, m * 2 * P + s * P), FB, P)

                if l % 2 == 0:
                    for half in range(2):
                        expert(a["w_ffn_gate"][l // 2], a["w_ffn_up"][l // 2],
                               a["w_ffn_down"][l // 2][half * F_EXP:(half + 1) * F_EXP, :], half * F_EXP)
                else:
                    with turns(sp, EXPERTS, {loads: EXPERT_UNITS}) as e:
                        pick = lambda w: w[l // 2, bass.ds(e, 1)].rearrange("o k n -> (o k) n")
                        expert(pick(a["w_exp_gate"]), pick(a["w_exp_up"]), pick(a["w_exp_down"]))
                for half in range(2):
                    load(cols(a["w_ple_proj"][l], 2, half * 4 * P, 4 * P), 2, 4 * P)
                with turns(sp, KC // 2, {loads: 2}) as m:
                    for s in range(2):
                        load(cols(a["w_ple_gate"][l], KC, m * 2 * P + s * P), KC, P)
            for b in range(TB):
                sp.wait_ge(out_ready, t.out_ready.next(2))
                sp.dma_start(out[0, b * P:(b + 1) * P, :], x_tok[:, b, :]).then_inc(out_landed, 16)
            sp.wait_ge(out_landed, 16 * TB)

        @block.gpsimd
        def _(pool):
            t = Tallies(sems)
            pool.nop().then_inc(lo_done, CREDIT)
            pool.nop().then_inc(staged, CREDIT)
            nc.gpsimd.memset(gate[:, 0:1], 0.0).then_inc(staged, t.staged.inc())
            slot = [0]

            def split_lo(n, width):
                pool.wait_ge(hi_done, t.hi_done.next())
                s = slot[0]
                nc.gpsimd.tensor_tensor(w_lo[:, s, 0:n * width], w_raw[:, s, 0:n * width],
                                               w_hi[:, s, 0:n * width].bitcast(F32), ALU.subtract).then_inc(lo_done, t.lo_done.inc())
                slot[0] = 1 - s

            def attention(pairs, n_rows):
                pool.wait_ge(q_ready, t.q_ready.now())
                pool.wait_ge(k_ready, t.k_ready.now())
                pool.wait_ge(rope_ready, t.rope_ready.now())
                pool.wait_ge(v_ready, t.v_ready.now())
                if n_rows == HD + 1:
                    pool.wait_ge(qrow_ready, t.qrow_ready.now())
                with turns(pool, pairs, {t.pv_done: 2, t.staged: 6}) as j:
                    for s in range(2):
                        pool.wait_ge(staged, t.staged.now())
                        pool.wait_ge(pv_done, t.pv_done.now(back=1))
                        nc.gpsimd.tensor_tensor(gate[:, 0:1], gate[:, 0:1], gate[:, 0:1], ALU.add).then_inc(staged, t.staged.inc())
                        nc.gpsimd.tensor_copy(q_st[0:n_rows, s, :], q_all[0:n_rows, j * 2 + s, :]).then_inc(staged, t.staged.inc())
                        nc.gpsimd.tensor_copy(v_st[:, s], v_all[:, :, bass.ds(j * P + s * HD, HD)]).then_inc(staged, t.staged.inc())
                        t.pv_done.add()

            for l in range(DEPTH):
                with turns(pool, 3, {t.hi_done: 2, t.lo_done: 2}):
                    split_lo(KC, P), split_lo(KC, P)
                for _ in range(4):
                    split_lo(KC, P)
                pool.wait_ge(negd_ready, t.negd_ready.next())
                pool.dma_start(k_all[HD:HD + 1, :, :], scan[:, 1, :]).then_inc(negd_landed, 16)
                t.q_ready.add(3), t.k_ready.add(3), t.v_ready.add(3), t.qrow_ready.add()
                attention(3, HD + 1)
                with turns(pool, 3, {t.hi_done: 2, t.lo_done: 2}):
                    split_lo(KC, P), split_lo(KC, P)
                for _ in range(3):
                    split_lo(KC, P)
                t.rope_ready.add(6), t.v_ready.add(3), t.qrow_ready.add()
                attention(3, HD + 1)
                for _ in range(5):
                    split_lo(KC, P)
                split_lo(2, MLA_HEADS * QK_M)
                split_lo(2, MLA_HEADS * P)
                t.rope_ready.add(1 + MLA_HEADS), t.v_ready.add(4), t.k_ready.add(4)
                attention(2, QK_M)
                with turns(pool, KC, {t.hi_done: 4, t.lo_done: 4}):
                    for _ in range(4):
                        split_lo(KC, P)
                with turns(pool, KC // 2, {t.hi_done: 2, t.lo_done: 2}):
                    split_lo(KC, P), split_lo(KC, P)
                with turns(pool, 2 if l % 2 == 0 else EXPERTS, {t.hi_done: EXPERT_UNITS, t.lo_done: EXPERT_UNITS}):
                    with turns(pool, FB, {t.hi_done: 2, t.lo_done: 2}):
                        split_lo(KC, P), split_lo(KC, P)
                    with turns(pool, KC // 2, {t.hi_done: 2, t.lo_done: 2}):
                        split_lo(FB, P), split_lo(FB, P)
                split_lo(2, 4 * P), split_lo(2, 4 * P)
                with turns(pool, KC // 2, {t.hi_done: 2, t.lo_done: 2}):
                    split_lo(KC, P), split_lo(KC, P)

        @block.tensor
        def _(pe):
            t = Tallies(sems)
            t.staged.add()
            pe.nop().then_inc(unit_done, CREDIT)
            pe.nop().then_inc(x_turns, CREDIT)
            pe.nop().then_inc(v_turns, CREDIT)
            pe.nop().then_inc(p_turns, CREDIT)
            pe.nop().then_inc(out_turns, CREDIT)
            pe.nop().then_inc(norm_mm, CREDIT)
            pe.nop().then_inc(rot_done, CREDIT)
            pe.nop().then_inc(s_done, CREDIT)
            pe.nop().then_inc(t_done, CREDIT)
            pe.nop().then_inc(pv_done, CREDIT)
            pe.nop().then_inc(route_done, CREDIT)
            slot = [0]

            def product(dst, s, cols, hi, lo, first=True, last=True):
                n, width = len(cols), dst.shape[0]
                for i, (c, k) in enumerate(cols):
                    wh, wl = w_hi[:, s, c:c + width], w_lo[:, s, c:c + width]
                    nc.tensor.matmul(dst, wh, hi[:, k, :], start=(first and i == 0), stop=False)
                    nc.tensor.matmul(dst, wh, lo[:, k, :], start=False, stop=False)
                    matmul = nc.tensor.matmul(dst, wl, hi[:, k, :], start=False, stop=(last and i == n - 1))
                return matmul

            def next_unit():
                pe.wait_ge(lo_done, t.lo_done.next())
                s = slot[0]
                slot[0] = 1 - s
                return s

            def block_cols(n):
                return [(k * P, k) for k in range(n)]

            def norm_sums(chunks, bank=7):
                for k in range(chunks):
                    pe.wait_ge(sq_ready, t.sq_ready.next())
                    nc.tensor.matmul(ps[:, bank, :], ones, sq[:, k % 2, :], start=(k == 0), stop=(k == chunks - 1)).then_inc(norm_mm, t.norm_mm.inc())

            def turn(dst_bank, src):
                for b in range(TB):
                    last = nc.tensor.transpose(ps[:, dst_bank, b * P:(b + 1) * P], src[:, b * P:(b + 1) * P], ident)
                return last

            def v_blocks(units):
                def turned(j):
                    pe.wait_ge(raw_ready, t.raw_ready.next())
                    if j >= 2:
                        pe.wait_ge(v_ready, t.v_ready.now(back=1))
                    turn(2 + j % 2, tmp[:, j % 2, :]).then_inc(v_turns, t.v_turns.inc())
                    t.v_ready.add()
                for j in range(units):
                    product(ps[:, j % 2, :], next_unit(), block_cols(KC), h_hi, h_lo).then_inc(unit_done, t.unit_done.inc())
                    if j:
                        turned(j - 1)
                turned(units - 1)

            def attention(pairs, n_rows):
                def scores(s, head):
                    pe.wait_ge(staged, t.staged.next(3))
                    for qb in range(TB):
                        pe.wait_ge(s_taken, t.s_taken.now(back=TB - 1))
                        nc.tensor.matmul(ps[:, qb, 0:(qb + 1) * P], q_st[0:n_rows, s, qb * P:(qb + 1) * P],
                                                k_all[0:n_rows, head, 0:(qb + 1) * P], start=True, stop=True).then_inc(s_done, t.s_done.inc())
                        t.s_taken.add()

                def turn_and_apply(s):
                    pe.wait_ge(p_ready, t.p_ready.next(TB))
                    for kb in range(TB):
                        evens = kb % 2 == 0
                        if evens:
                            pe.wait_ge(pt_even, t.pt_even.now())
                        else:
                            pe.wait_ge(pt_odd, t.pt_odd.now())
                        for qb in range(kb, TB):
                            last = nc.tensor.transpose(ps[:, 4 + kb % 2, (qb - kb) * P:(qb - kb + 1) * P],
                                                       probs[:, s, qb, kb * P:(kb + 1) * P], ident)
                        last.then_inc(t_done, t.t_done.inc())
                        (t.pt_even if evens else t.pt_odd).add()
                        if kb >= 1:
                            values(s, kb - 1)
                    values(s, TB - 1)

                def values(s, kb):
                    if kb % 2 == 0:
                        pe.wait_ge(pt_even, t.pt_even.now())
                    else:
                        pe.wait_ge(pt_odd, t.pt_odd.now())
                    if kb == 0 and s == 0:
                        pe.wait_ge(olo_ready, t.olo_ready.now())
                    n = (TB - kb) * P
                    o = kb * TB * P - kb * (kb - 1) // 2 * P
                    last = nc.tensor.matmul(ps[s * HD:(s + 1) * HD, 6, kb * P:T], v_st[:, s, kb, :],
                                            pt[:, o:o + n], start=(kb == 0), stop=(kb == TB - 1), skip_group_check=True)
                    if kb == TB - 1:
                        last.then_inc(pv_done, t.pv_done.inc())

                def pair(j, last):
                    scores(1, j * 2 + 1)
                    turn_and_apply(0)
                    if not last:
                        scores(0, j * 2 + 2)
                    turn_and_apply(1)
                    t.olo_ready.add()

                pe.wait_ge(rope_ready, t.rope_ready.now())
                pe.wait_ge(q_ready, t.q_ready.now())
                pe.wait_ge(k_ready, t.k_ready.now())
                scores(0, 0)
                with turns(pe, pairs - 1, {t.staged: 6, t.s_taken: 8, t.s_done: 8, t.p_ready: 8, t.pt_even: 4,
                                           t.pt_odd: 4, t.t_done: 8, t.pv_done: 2, t.olo_ready: 1}) as j:
                    pair(j, False)
                pair(pairs - 1, True)
                pe.wait_ge(s_taken, t.s_taken.now())
                pe.wait_ge(olo_ready, t.olo_ready.now())

            pe.wait_ge(x_landed, 16)
            pe.wait_ge(setup_landed, SETUP_LANDED)
            for k in range(KC):
                if k >= 2:
                    pe.wait_ge(x_turned, t.x_turned.now(back=1))
                for b in range(TB):
                    last = nc.tensor.transpose(ps[:, k % 2, b * P:(b + 1) * P], x_tok[:, b, k * P:(k + 1) * P], ident)
                last.then_inc(x_turns, t.x_turns.inc())
                t.x_turned.add()
            pe.wait_ge(x_turned, t.x_turned.now())

            for l in range(DEPTH):
                norm_sums(KC)
                pe.wait_ge(hlo_ready, t.hlo_ready.next(KC))
                with turns(pe, 3, {t.lo_done: 2, t.unit_done: 2, t.q_ready: 1, t.k_ready: 1}):
                    pe.wait_ge(q_ready, t.q_ready.now())
                    product(ps[:, 0, :], next_unit(), block_cols(KC), h_hi, h_lo).then_inc(unit_done, t.unit_done.inc())
                    t.q_ready.add()
                    pe.wait_ge(k_ready, t.k_ready.now())
                    product(ps[:, 1, :], next_unit(), block_cols(KC), h_hi, h_lo).then_inc(unit_done, t.unit_done.inc())
                    t.k_ready.add()
                pe.wait_ge(q_ready, t.q_ready.now())
                pe.wait_ge(k_ready, t.k_ready.now())
                v_blocks(3)
                product(ps[:, 5, :], next_unit(), block_cols(KC), h_hi, h_lo).then_inc(unit_done, t.unit_done.inc())
                pe.wait_ge(v_ready, t.v_ready.now())
                pe.wait_ge(fz_taken, t.fz_taken.next())
                pe.wait_ge(negd_landed, 16 * (l + 1))
                pe.wait_ge(qrow_ready, t.qrow_ready.next())
                attention(3, HD + 1)
                with turns(pe, 3, {t.lo_done: 2, t.unit_done: 2, t.raw_ready: 2, t.rot_done: 2, t.rope_ready: 2}):
                    pe.wait_ge(raw_ready, t.raw_ready.now())
                    for s in range(2):
                        product(ps[:, s, :], next_unit(), block_cols(KC), h_hi, h_lo).then_inc(unit_done, t.unit_done.inc())
                    for s in range(2):
                        pe.wait_ge(raw_ready, t.raw_ready.next())
                        pe.wait_ge(rope_ready, t.rope_ready.now(back=s))
                        nc.tensor.matmul(ps[:, 2 + s, :], rot_d, tmp[:, s, :], start=True, stop=True).then_inc(rot_done, t.rot_done.inc())
                        t.rope_ready.add()
                pe.wait_ge(rope_ready, t.rope_ready.now())
                v_blocks(3)
                pe.wait_ge(v_ready, t.v_ready.now())
                pe.wait_ge(qrow_ready, t.qrow_ready.next())
                attention(3, HD + 1)
                for n in range(5):
                    product(ps[:, n, :], next_unit(), block_cols(KC), h_hi, h_lo).then_inc(unit_done, t.unit_done.inc())
                pe.wait_ge(raw_ready, t.raw_ready.next())
                nc.tensor.matmul(ps[0:QK_M, 5, :], rot_m, tmp[0:QK_M, 0, :], start=True, stop=True).then_inc(rot_done, t.rot_done.inc())
                t.rope_ready.add()
                norm_sums(2)
                pe.wait_ge(hlo_ready, t.hlo_ready.next(2))
                s = next_unit()
                for hd in range(MLA_HEADS):
                    last = product(ps[0:QK_M, hd, :], s, [(k * MLA_HEADS * QK_M + hd * QK_M, k) for k in range(2)], cn_hi, cn_lo)
                last.then_inc(unit_done, t.unit_done.inc())
                for hd in range(MLA_HEADS):
                    pe.wait_ge(raw_ready, t.raw_ready.next())
                    pe.wait_ge(rope_ready, t.rope_ready.now(back=min(hd, 1)))
                    nc.tensor.matmul(ps[0:QK_M, 5 + hd % 2, :], rot_m, tmp[0:QK_M, hd % 2, :], start=True, stop=True).then_inc(rot_done, t.rot_done.inc())
                    t.rope_ready.add()
                norm_sums(2)
                pe.wait_ge(hlo_ready, t.hlo_ready.next(2))
                s = next_unit()
                for hd in range(MLA_HEADS):
                    last = product(ps[:, hd, :], s, [(k * MLA_HEADS * P + hd * P, k) for k in range(2)], cn_hi, cn_lo)
                last.then_inc(unit_done, t.unit_done.inc())
                pe.wait_ge(rope_ready, t.rope_ready.now())
                for hd in range(MLA_HEADS):
                    pe.wait_ge(raw_ready, t.raw_ready.next())
                    if hd >= 2:
                        pe.wait_ge(v_ready, t.v_ready.now(back=1))
                    turn(4 + hd % 2, tmp[:, hd % 2, :]).then_inc(v_turns, t.v_turns.inc())
                    t.v_ready.add()
                t.k_ready.add(4)
                pe.wait_ge(v_ready, t.v_ready.now())
                attention(2, QK_M)
                with turns(pe, KC, {t.lo_done: 4, t.unit_done: 4, t.sig_ready: 3, t.mlo_ready: 1}):
                    for b in range(3):
                        pe.wait_ge(sig_ready, t.sig_ready.now(back=2))
                        product(ps[:, b, :], next_unit(), block_cols(KC), h_hi, h_lo).then_inc(unit_done, t.unit_done.inc())
                        t.sig_ready.add()
                    s = next_unit()
                    pe.wait_ge(mlo_ready, t.mlo_ready.now())
                    for b, (c0, c1) in enumerate(((0, 3), (3, 6), (6, 8))):
                        last = product(ps[:, 3 + b, :], s, [(c * P, c) for c in range(c0, c1)], o_hi, o_lo)
                    last.then_inc(unit_done, t.unit_done.inc())
                    t.mlo_ready.add()
                with turns(pe, KC // 2, {t.lo_done: 2, t.unit_done: 2, t.x_upd: 2}):
                    for s in range(2):
                        pe.wait_ge(mlo_ready, t.mlo_ready.now(back=1))
                        pe.wait_ge(x_upd, t.x_upd.now(back=1))
                        unit = next_unit()
                        product(ps[:, 6 + s, :], unit, block_cols(KC)[:-1], m_hi, m_lo, last=False)
                        pe.wait_ge(mlo_ready, t.mlo_ready.now())
                        product(ps[:, 6 + s, :], unit, block_cols(KC)[-1:], m_hi, m_lo, first=False).then_inc(unit_done, t.unit_done.inc())
                        t.x_upd.add()
                pe.wait_ge(x_upd, t.x_upd.now())
                norm_sums(KC)
                pe.wait_ge(p_landed, 16 * (l + 1))
                for c in range(PLE // P):
                    for b in range(TB):
                        last = nc.tensor.transpose(ps[:, 4 + c, b * P:(b + 1) * P], p_tok[:, b, c * P:(c + 1) * P], ident)
                    last.then_inc(p_turns, t.p_turns.inc())
                t.plo_ready.add(2)
                pe.wait_ge(hlo_ready, t.hlo_ready.next(KC))

                def expert(sparse):
                    with turns(pe, FB, {t.lo_done: 2, t.unit_done: 2, t.sig_ready: 1, t.alo_ready: 1}):
                        pe.wait_ge(sig_ready, t.sig_ready.now())
                        product(ps[:, 0, :], next_unit(), block_cols(KC), h_hi, h_lo).then_inc(unit_done, t.unit_done.inc())
                        t.sig_ready.add()
                        pe.wait_ge(alo_ready, t.alo_ready.now())
                        product(ps[:, 1, :], next_unit(), block_cols(KC), h_hi, h_lo).then_inc(unit_done, t.unit_done.inc())
                        t.alo_ready.add()
                    if sparse:
                        pe.wait_ge(comb_ready, t.comb_ready.next())
                        pe.wait_ge(plo_ready, t.plo_ready.now())
                        nc.tensor.matmul(ps[:, 4, :], ones[0:EXPERTS, :], comb_t[:, 1, :], start=True, stop=True).then_inc(route_done, t.route_done.inc())
                    with turns(pe, KC // 2, {t.lo_done: 2, t.unit_done: 2, t.x_upd: 2}):
                        for s in range(2):
                            pe.wait_ge(alo_ready, t.alo_ready.now(back=1))
                            pe.wait_ge(x_upd, t.x_upd.now(back=1))
                            unit = next_unit()
                            product(ps[:, 2 + s, :], unit, block_cols(FB)[:-1], a_hi, a_lo, last=False)
                            pe.wait_ge(alo_ready, t.alo_ready.now())
                            product(ps[:, 2 + s, :], unit, block_cols(FB)[-1:], a_hi, a_lo, first=False).then_inc(unit_done, t.unit_done.inc())
                            t.x_upd.add()

                if l % 2 == 0:
                    expert_per = {t.lo_done: EXPERT_UNITS, t.unit_done: EXPERT_UNITS, t.sig_ready: FB, t.alo_ready: FB, t.x_upd: KC}
                    with turns(pe, 2, expert_per):
                        expert(False)
                else:
                    pe.wait_ge(wr_ready, t.wr_ready.next())
                    for b in range(TB):
                        for k in range(KC):
                            for i, (hh, ww) in enumerate(((h_hi, wr_hi), (h_hi, wr_lo), (h_lo, wr_hi))):
                                last = nc.tensor.matmul(ps[:, 6, b * EXPERTS:(b + 1) * EXPERTS], hh[:, k, b * P:(b + 1) * P],
                                                        ww[:, k, :], start=(k == 0 and i == 0), stop=(k == KC - 1 and i == 2))
                    last.then_inc(route_done, t.route_done.inc())
                    pe.wait_ge(comb_ready, t.comb_ready.next())
                    for b in range(TB):
                        last = nc.tensor.transpose(ps[0:EXPERTS, 7, b * P:(b + 1) * P], route[:, 11, b, :], ident)
                    last.then_inc(route_done, t.route_done.inc())
                    expert_per = {t.lo_done: EXPERT_UNITS, t.unit_done: EXPERT_UNITS, t.sig_ready: FB, t.alo_ready: FB,
                                  t.x_upd: KC, t.comb_ready: 1, t.route_done: 1}
                    with turns(pe, EXPERTS, expert_per):
                        expert(True)
                pe.wait_ge(x_upd, t.x_upd.now())
                pe.wait_ge(plo_ready, t.plo_ready.now())
                for half in range(2):
                    s = next_unit()
                    pe.wait_ge(pp_ready, t.pp_ready.now())
                    for n in range(4):
                        last = product(ps[:, n, :], s, [(c * 4 * P + n * P, c) for c in range(2)], p_hi, p_lo)
                    last.then_inc(unit_done, t.unit_done.inc())
                    t.pp_ready.add(4)
                norm_sums(KC)
                pe.wait_ge(hlo_ready, t.hlo_ready.next(KC))
                with turns(pe, KC // 2, {t.lo_done: 2, t.unit_done: 2, t.x_upd: 2}):
                    for s in range(2):
                        pe.wait_ge(x_upd, t.x_upd.now(back=1))
                        product(ps[:, 4 + s, :], next_unit(), block_cols(KC), h_hi, h_lo).then_inc(unit_done, t.unit_done.inc())
                        t.x_upd.add()
                pe.wait_ge(x_upd, t.x_upd.now())
                t.sig_ready.add(KC)
            norm_sums(KC)
            pe.wait_ge(xn_ready, t.xn_ready.next(KC))
            for b in range(TB):
                for half in range(2):
                    pe.wait_ge(out_ready, t.out_ready.now(back=1))
                    for k in range(KC // 2):
                        last = nc.tensor.transpose(ps[:, half, k * P:(k + 1) * P], x[:, half * KC // 2 + k, b * P:(b + 1) * P], ident)
                    last.then_inc(out_turns, t.out_turns.inc())
                    t.out_ready.add()

        @block.scalar
        def _(act):
            t = Tallies(sems)
            act.nop().then_inc(hi_done, CREDIT)
            act.nop().then_inc(act_step, CREDIT)
            act.nop().then_inc(sq_ready, CREDIT)
            act.nop().then_inc(root_ready, CREDIT)
            act.nop().then_inc(hn_ready, CREDIT)
            act.nop().then_inc(raw_ready, CREDIT)
            act.nop().then_inc(k_ready, CREDIT)
            act.nop().then_inc(sig_ready, CREDIT)
            act.nop().then_inc(mhi_ready, CREDIT)
            act.nop().then_inc(ahi_ready, CREDIT)
            act.nop().then_inc(exp_done, CREDIT)
            act.nop().then_inc(pt_even, CREDIT)
            act.nop().then_inc(ohi_ready, CREDIT)
            act.nop().then_inc(fz_ready, CREDIT)
            act.nop().then_inc(phi_ready, CREDIT)
            act.nop().then_inc(pp_ready, CREDIT)
            act.nop().then_inc(share_ready, CREDIT)
            landed = [t.w_landed0, t.w_landed1]
            slot = [0]
            A = nc.scalar.activation

            def split_hi(dmas=1):
                s = slot[0]
                landed[s].add(16 * dmas)
                act.wait_ge(landed[s].sem, landed[s].now())
                act.wait_ge(unit_done, t.hi_done.now(back=1))
                A(w_hi[:, s, :], w_raw[:, s, :], ACT.Copy).then_inc(hi_done, t.hi_done.inc())
                slot[0] = 1 - s

            def norm(src, chunks, bank, dim):
                for k in range(chunks):
                    act.wait_ge(norm_mm, t.norm_mm.now(back=1))
                    A(sq[:, k % 2, :], src[:, k, :], ACT.Square).then_inc(sq_ready, t.sq_ready.inc())
                    t.norm_mm.add()
                act.wait_ge(norm_mm, t.norm_mm.now())
                A(rstd[:], ps[:, bank, :], ACT.Sqrt, bias=const[:, K_EPS:K_EPS + 1], scale=1.0 / dim).then_inc(root_ready, t.root_ready.inc())

            def norm_hi(chunks, hi):
                for k in range(chunks):
                    act.wait_ge(hf_ready, t.hf_ready.next())
                    A(hi[:, k, :], tmp[:, 2 + k % 2, :], ACT.Copy).then_inc(hn_ready, t.hn_ready.inc())

            def v_blocks(units):
                for j in range(units):
                    split_hi()
                    act.wait_ge(unit_done, t.unit_done.next())
                    act.wait_ge(v_turns, t.v_turns.now(back=min(j, 1)))
                    A(tmp[:, j % 2, :], ps[:, j % 2, :], ACT.Copy).then_inc(raw_ready, t.raw_ready.inc())
                    t.v_turns.add()

            def attention(pairs, pair0):
                def exponentials(s):
                    act.wait_ge(neg_ready, t.neg_ready.next())
                    for qb in range(TB):
                        n = (qb + 1) * P
                        A(probs[:, s, qb, 0:n], probs[:, s, qb, 0:n], ACT.Exp, bias=sneg[:, s, qb:qb + 1],
                                 accum_out=ssum[:, s, qb:qb + 1]).then_inc(exp_done, t.exp_done.inc())

                def even_blocks(s):
                    for kb in range(0, TB, 2):
                        act.wait_ge(t_done, t.t_done.next())
                        act.wait_ge(pv_done, t.pv_done.now())
                        n, o = (TB - kb) * P, kb * TB * P - kb * (kb - 1) // 2 * P
                        A(pt[:, o:o + n], ps[:, 4, 0:n], ACT.Copy).then_inc(pt_even, t.pt_even.inc())
                        t.t_done.add()
                    t.pv_done.add()

                def pair(j, last):
                    exponentials(1)
                    even_blocks(0)
                    if not last:
                        exponentials(0)
                    even_blocks(1)
                    act.wait_ge(pv_done, t.pv_done.now())
                    A(o_hi[:, pair0 + j, :], ps[:, 6, :], ACT.Copy).then_inc(ohi_ready, t.ohi_ready.inc())

                exponentials(0)
                with turns(act, pairs - 1, {t.neg_ready: 2, t.exp_done: 8, t.t_done: 8, t.pv_done: 2, t.pt_even: 4,
                                            t.ohi_ready: 1}) as j:
                    pair(j, False)
                pair(pairs - 1, True)

            for n, (cos_t, sin_t) in enumerate(((cos_d, sin_d), (cos_m, sin_m))):
                act.wait_ge(ang_ready, t.ang_ready.next())
                A(sin_t[:], trig[:, n, :], ACT.Sin)
                A(trig[:, 2 + n, :], trig[:, n, :], ACT.Abs).then_inc(act_step, t.act_step.inc())
                act.wait_ge(act_step, t.act_step.now())
                A(cos_t[:], trig[:, 2 + n, :], ACT.Sin, scale=-1.0, bias=const[:, K_HALFPI:K_HALFPI + 1]).then_inc(act_step, t.act_step.inc())
            act.wait_ge(x_turned, t.x_turned.next(KC))
            for _ in range(2):
                split_hi()

            for l in range(DEPTH):
                last_layer = l == DEPTH - 1
                norm(x, KC, 7, D)
                norm_hi(KC, h_hi)
                with turns(act, 3, {t.hi_done: 2, t.w_landed0: 16, t.w_landed1: 16, t.unit_done: 2, t.k_ready: 1}) as j:
                    split_hi()
                    t.unit_done.add()
                    split_hi()
                    act.wait_ge(unit_done, t.unit_done.next())
                    A(k_all[0:HD, j * 2, :], ps[0:HD, 1, :], ACT.Copy)
                    A(k_all[0:HD, j * 2 + 1, :], ps[HD:P, 1, :], ACT.Copy).then_inc(k_ready, t.k_ready.inc())
                v_blocks(3)
                split_hi()
                t.unit_done.add()
                act.wait_ge(fz_taken, t.fz_taken.next())
                A(scan_t[:, 1, :], scan_t[:, 0, :], ACT.Abs).then_inc(act_step, t.act_step.inc())
                act.wait_ge(act_step, t.act_step.now())
                A(scan_t[:, 2, :], scan_t[:, 1, :], ACT.Exp, scale=-1.0).then_inc(act_step, t.act_step.inc())
                act.wait_ge(act_step, t.act_step.now())
                A(scan_t[:, 3, :], scan_t[:, 2, :], ACT.Ln, bias=1.0).then_inc(fz_ready, t.fz_ready.inc())
                attention(3, 0)
                with turns(act, 3, {t.hi_done: 2, t.w_landed0: 16, t.w_landed1: 16, t.unit_done: 2, t.raw_ready: 2, t.rope_ready: 2}):
                    for s in range(2):
                        split_hi()
                        act.wait_ge(unit_done, t.unit_done.next())
                        act.wait_ge(rope_ready, t.rope_ready.now(back=s))
                        A(tmp[:, s, :], ps[:, s, :], ACT.Copy, scale=HD**-0.5 if s == 0 else 1.0).then_inc(raw_ready, t.raw_ready.inc())
                    t.rope_ready.add(2)
                act.wait_ge(rope_ready, t.rope_ready.now())
                v_blocks(3)
                attention(3, 3)
                for n in range(5):
                    split_hi()
                    act.wait_ge(unit_done, t.unit_done.next())
                    if n == 4:
                        act.wait_ge(v_turns, t.v_turns.now())
                        A(tmp[0:QK_M, 0, :], ps[0:QK_M, 4, :], ACT.Copy).then_inc(raw_ready, t.raw_ready.inc())
                    else:
                        dst = cq_raw if n < 2 else ckv_raw
                        A(dst[:, n % 2, :], ps[:, n, :], ACT.Copy).then_inc(act_step, t.act_step.inc())
                act.wait_ge(act_step, t.act_step.now())
                norm(cq_raw, 2, 7, RANK)
                norm_hi(2, cn_hi)
                split_hi()
                act.wait_ge(unit_done, t.unit_done.next())
                t.rope_ready.add()
                for hd in range(MLA_HEADS):
                    act.wait_ge(rope_ready, t.rope_ready.now(back=min(hd, 1)))
                    A(tmp[0:QK_M, hd % 2, :], ps[0:QK_M, hd, :], ACT.Copy, scale=QK_M**-0.5).then_inc(raw_ready, t.raw_ready.inc())
                    t.rope_ready.add()
                norm(ckv_raw, 2, 7, RANK)
                norm_hi(2, cn_hi)
                split_hi()
                act.wait_ge(unit_done, t.unit_done.next())
                act.wait_ge(rope_ready, t.rope_ready.now())
                for hd in range(MLA_HEADS):
                    A(k_all[0:NOPE, hd, :], ps[0:NOPE, hd, :], ACT.Copy).then_inc(k_ready, t.k_ready.inc())
                    act.wait_ge(v_turns, t.v_turns.now(back=min(hd, 1)))
                    A(tmp[:, hd % 2, :], ps[:, hd, :], ACT.Copy).then_inc(raw_ready, t.raw_ready.inc())
                    t.v_turns.add()
                attention(2, 6)
                with turns(act, KC, {t.hi_done: 4, t.w_landed0: 32, t.w_landed1: 64, t.unit_done: 4, t.sig_ready: 3,
                                     t.m_ready: 1, t.mhi_ready: 1, t.mlo_ready: 1}) as m:
                    for b in range(3):
                        split_hi(3 if b == 1 else 1)
                        act.wait_ge(unit_done, t.unit_done.next())
                        act.wait_ge(mlo_ready, t.mlo_ready.now())
                        A(sg[:, b, :], ps[:, b, :], ACT.Sigmoid).then_inc(sig_ready, t.sig_ready.inc())
                    split_hi()
                    t.unit_done.add()
                    act.wait_ge(m_ready, t.m_ready.next())
                    A(m_hi[:, m, :], tmp[:, 0, :], ACT.Copy).then_inc(mhi_ready, t.mhi_ready.inc())
                    t.mlo_ready.add()
                with turns(act, KC // 2, {t.hi_done: 2, t.w_landed0: 16, t.w_landed1: 16, t.unit_done: 2}):
                    for s in range(2):
                        split_hi()
                        t.unit_done.add()
                act.wait_ge(x_upd, t.x_upd.next(KC))
                norm(x, KC, 7, D)
                for c in range(PLE // P):
                    act.wait_ge(p_turns, t.p_turns.next())
                    A(p_hi[:, c, :], ps[:, 4 + c, :], ACT.Copy).then_inc(phi_ready, t.phi_ready.inc())
                norm_hi(KC, h_hi)
                experts = 2 if l % 2 == 0 else EXPERTS
                if l % 2:
                    act.wait_ge(gap_ready, t.gap_ready.next())
                    A(route[:, 9, :, 0:1], route[:, 8, :, 0:1], ACT.Exp).then_inc(share_ready, t.share_ready.inc())
                with turns(act, experts, {t.hi_done: EXPERT_UNITS, t.w_landed0: 8 * EXPERT_UNITS, t.w_landed1: 8 * EXPERT_UNITS,
                                          t.unit_done: EXPERT_UNITS, t.af_ready: FB, t.sig_ready: FB, t.ahi_ready: FB}):
                    with turns(act, FB, {t.hi_done: 2, t.w_landed0: 16, t.w_landed1: 16, t.unit_done: 2, t.af_ready: 1,
                                         t.sig_ready: 1, t.ahi_ready: 1}) as f:
                        split_hi()
                        act.wait_ge(unit_done, t.unit_done.next())
                        act.wait_ge(af_ready, t.af_ready.now())
                        A(sg[:, 0, :], ps[:, 0, :], ACT.Silu).then_inc(sig_ready, t.sig_ready.inc())
                        split_hi()
                        t.unit_done.add()
                        act.wait_ge(af_ready, t.af_ready.next())
                        A(a_hi[:, f, :], tmp[:, 0, :], ACT.Copy).then_inc(ahi_ready, t.ahi_ready.inc())
                    with turns(act, KC // 2, {t.hi_done: 2, t.w_landed0: 16, t.w_landed1: 16, t.unit_done: 2}):
                        for s in range(2):
                            split_hi()
                            t.unit_done.add()
                for half in range(2):
                    split_hi()
                    act.wait_ge(unit_done, t.unit_done.next())
                    for n in range(4):
                        A(pp[:, half * 4 + n, :], ps[:, n, :], ACT.Copy).then_inc(pp_ready, t.pp_ready.inc())
                act.wait_ge(x_upd, t.x_upd.next(KC * experts))
                norm(x, KC, 7, D)
                norm_hi(KC, h_hi)

                def gates(split):
                    for s in range(2):
                        if split:
                            split_hi()
                        act.wait_ge(unit_done, t.unit_done.next())
                        act.wait_ge(x_upd, t.x_upd.now(back=1))
                        A(sg[:, s, :], ps[:, 4 + s, :], ACT.Sigmoid).then_inc(sig_ready, t.sig_ready.inc())
                        t.x_upd.add()

                gate_turns = KC // 2 - last_layer
                with turns(act, gate_turns, {t.hi_done: 2, t.w_landed0: 16, t.w_landed1: 16, t.unit_done: 2, t.x_upd: 2, t.sig_ready: 2}):
                    gates(True)
                if last_layer:
                    gates(False)
                act.wait_ge(x_upd, t.x_upd.now())
            norm(x, KC, 7, D)

        @block.vector
        def _(dve):
            t = Tallies(sems)
            dve.nop().then_inc(dve_step, CREDIT)
            dve.nop().then_inc(raw_zeroed, CREDIT)
            dve.nop().then_inc(x_turned, CREDIT)
            dve.nop().then_inc(ang_ready, CREDIT)
            dve.nop().then_inc(hf_ready, CREDIT)
            dve.nop().then_inc(hlo_ready, CREDIT)
            dve.nop().then_inc(q_ready, CREDIT)
            dve.nop().then_inc(rope_ready, CREDIT)
            dve.nop().then_inc(v_ready, CREDIT)
            dve.nop().then_inc(fz_taken, CREDIT)
            dve.nop().then_inc(negd_ready, CREDIT)
            dve.nop().then_inc(s_taken, CREDIT)
            dve.nop().then_inc(neg_ready, CREDIT)
            dve.nop().then_inc(p_ready, CREDIT)
            dve.nop().then_inc(pt_odd, CREDIT)
            dve.nop().then_inc(olo_ready, CREDIT)
            dve.nop().then_inc(m_ready, CREDIT)
            dve.nop().then_inc(mlo_ready, CREDIT)
            dve.nop().then_inc(x_upd, CREDIT)
            dve.nop().then_inc(af_ready, CREDIT)
            dve.nop().then_inc(alo_ready, CREDIT)
            dve.nop().then_inc(plo_ready, CREDIT)
            dve.nop().then_inc(out_ready, CREDIT)
            dve.nop().then_inc(xn_ready, CREDIT)
            dve.nop().then_inc(comb_ready, CREDIT)
            dve.nop().then_inc(wr_ready, CREDIT)
            dve.nop().then_inc(qrow_ready, CREDIT)
            dve.nop().then_inc(gap_ready, CREDIT)
            V = nc.vector

            def norm(src, chunks, gain, hi, lo):
                dve.wait_ge(root_ready, t.root_ready.next())
                V.reciprocal(rstd[:], rstd[:]).then_inc(dve_step, t.dve_step.inc())
                dve.wait_ge(dve_step, t.dve_step.now())

                def lower(k):
                    dve.wait_ge(hn_ready, t.hn_ready.next())
                    V.tensor_tensor(lo[:, k, :], tmp[:, 2 + k % 2, :], hi[:, k, :].bitcast(F32), ALU.subtract).then_inc(hlo_ready, t.hlo_ready.inc())
                for k in range(chunks):
                    dve.wait_ge(hlo_ready, t.hlo_ready.now())
                    V.scalar_tensor_tensor(out=tmp[:, 2 + k % 2, :], in0=src[:, k, :], scalar=gain[:, k:k + 1],
                                                  in1=rstd[:], op0=ALU.mult, op1=ALU.mult).then_inc(hf_ready, t.hf_ready.inc())
                    if k:
                        dve.wait_ge(hf_ready, t.hf_ready.now(back=1))
                        lower(k - 1)
                dve.wait_ge(hf_ready, t.hf_ready.now())
                lower(chunks - 1)

            def rope(s, bank, n_rows, cos_t, sin_t, outs):
                dve.wait_ge(raw_ready, t.raw_ready.next())
                dve.wait_ge(rope_ready, t.rope_ready.now())
                V.tensor_tensor(tmp[0:n_rows, 2, :], tmp[0:n_rows, s, :], cos_t[0:n_rows, :], ALU.mult)
                dve.wait_ge(rot_done, t.rot_done.next())
                V.tensor_tensor(tmp[0:n_rows, 3, :], ps[0:n_rows, bank, :], sin_t[0:n_rows, :], ALU.mult).then_inc(dve_step, t.dve_step.inc())
                dve.wait_ge(dve_step, t.dve_step.now())
                for dst, r0, r1 in outs:
                    last = V.tensor_tensor(dst, tmp[r0:r1, 2, :], tmp[r0:r1, 3, :], ALU.add)
                last.then_inc(rope_ready, t.rope_ready.inc())

            def v_blocks(units):
                for j in range(units):
                    t.unit_done.add(), t.raw_ready.add()
                    dve.wait_ge(v_turns, t.v_turns.next())
                    V.tensor_copy(v_all[:, :, j * P:(j + 1) * P],
                                         ps[:, 2 + j % 2, :].rearrange("p (b n) -> p b n", b=TB)).then_inc(v_ready, t.v_ready.inc())

            def attention(pairs, pair0, kind):
                def maxima(s):
                    for qb in range(TB):
                        n = (qb + 1) * P
                        dve.wait_ge(s_done, t.s_done.next())
                        V.memset(gate[:, 4 + s * TB + qb:5 + s * TB + qb], 0.0)
                        V.tensor_tensor_reduce(out=probs[:, s, qb, 0:n], in0=ps[:, qb, 0:n],
                                                      in1=const[:, K_BIAS + kind * T + T - n:K_BIAS + (kind + 1) * T],
                                                      scale=1.0, scalar=-3e38, op0=ALU.add, op1=ALU.max,
                                                      accum_out=smax[:, s, qb:qb + 1]).then_inc(s_taken, t.s_taken.inc())
                    dve.wait_ge(s_taken, t.s_taken.now())
                    V.tensor_scalar(sneg[:, s, :], smax[:, s, :], -1.0, None, ALU.mult).then_inc(neg_ready, t.neg_ready.inc())

                def normalise(s):
                    dve.wait_ge(exp_done, t.exp_done.next(TB))
                    V.reciprocal(srec[:, s, :], ssum[:, s, :]).then_inc(dve_step, t.dve_step.inc())
                    dve.wait_ge(dve_step, t.dve_step.now())
                    for qb in range(TB):
                        n = (qb + 1) * P
                        V.tensor_scalar(probs[:, s, qb, 0:n], probs[:, s, qb, 0:n], srec[:, s, qb:qb + 1], None, ALU.mult).then_inc(p_ready, t.p_ready.inc())

                def odd_blocks(s):
                    for kb in range(1, TB, 2):
                        t.t_done.add()
                        dve.wait_ge(t_done, t.t_done.next())
                        dve.wait_ge(pv_done, t.pv_done.now())
                        n, o = (TB - kb) * P, kb * TB * P - kb * (kb - 1) // 2 * P
                        V.tensor_copy(pt[:, o:o + n], ps[:, 5, 0:n]).then_inc(pt_odd, t.pt_odd.inc())
                    t.pv_done.add()

                def pair(j, last):
                    normalise(0)
                    maxima(1)
                    odd_blocks(0)
                    normalise(1)
                    if not last:
                        maxima(0)
                    odd_blocks(1)
                    dve.wait_ge(ohi_ready, t.ohi_ready.next())
                    V.tensor_tensor(o_lo[:, pair0 + j, :], ps[:, 6, :], o_hi[:, pair0 + j, :].bitcast(F32), ALU.subtract).then_inc(olo_ready, t.olo_ready.inc())

                maxima(0)
                with turns(dve, pairs - 1, {t.s_done: 8, t.s_taken: 8, t.neg_ready: 2, t.exp_done: 8, t.dve_step: 2, t.p_ready: 8,
                                            t.t_done: 8, t.pv_done: 2, t.pt_odd: 4, t.ohi_ready: 1, t.olo_ready: 1}) as j:
                    pair(j, False)
                pair(pairs - 1, True)

            def routing():
                r = lambda n, b: route[:, n, b, :]
                V.tensor_copy(route[:, 0], ps[:, 6, 0:TB * EXPERTS].rearrange("p (b e) -> p b e", b=TB)).then_inc(dve_step, t.dve_step.inc())
                dve.wait_ge(dve_step, t.dve_step.now())
                iota = const[:, K_IOTA:K_IOTA + EXPERTS]
                for b in range(TB):
                    for n, src in ((1, 0), (2, 5)):
                        V.max(out=r(n, b), in_=r(src, b)).then_inc(dve_step, t.dve_step.inc())
                        dve.wait_ge(dve_step, t.dve_step.now())
                        V.max_index(out=route_i[:, b, :], in_max=r(n, b), in_values=r(src, b)).then_inc(dve_step, t.dve_step.inc())
                        dve.wait_ge(dve_step, t.dve_step.now())
                        index, hot = (3, 4) if n == 1 else (6, 7)
                        V.tensor_copy(r(index, b), route_i[:, b, :]).then_inc(dve_step, t.dve_step.inc())
                        dve.wait_ge(dve_step, t.dve_step.now())
                        V.tensor_scalar(r(hot, b), iota, r(index, b)[:, 0:1], None, ALU.is_equal).then_inc(dve_step, t.dve_step.inc())
                        dve.wait_ge(dve_step, t.dve_step.now())
                        if n == 1:
                            V.scalar_tensor_tensor(out=r(5, b), in0=r(4, b), scalar=MASKED, in1=r(0, b), op0=ALU.mult, op1=ALU.add).then_inc(dve_step, t.dve_step.inc())
                            dve.wait_ge(dve_step, t.dve_step.now())
                V.tensor_tensor(route[:, 8, :, 0:1], route[:, 2, :, 0:1], route[:, 1, :, 0:1], ALU.subtract).then_inc(gap_ready, t.gap_ready.inc())
                dve.wait_ge(share_ready, t.share_ready.next())
                V.tensor_scalar(route[:, 8, :, 1:2], route[:, 9, :, 0:1], 1.0, None, ALU.add).then_inc(dve_step, t.dve_step.inc())
                dve.wait_ge(dve_step, t.dve_step.now())
                V.reciprocal(route[:, 10, :, 0:1], route[:, 8, :, 1:2]).then_inc(dve_step, t.dve_step.inc())
                dve.wait_ge(dve_step, t.dve_step.now())
                V.tensor_tensor(route[:, 10, :, 1:2], route[:, 10, :, 0:1], route[:, 9, :, 0:1], ALU.mult).then_inc(dve_step, t.dve_step.inc())
                dve.wait_ge(dve_step, t.dve_step.now())
                for b in range(TB):
                    V.tensor_scalar(r(11, b), r(7, b), r(10, b)[:, 1:2], None, ALU.mult).then_inc(dve_step, t.dve_step.inc())
                    dve.wait_ge(dve_step, t.dve_step.now())
                    last = V.scalar_tensor_tensor(out=r(11, b), in0=r(4, b), scalar=r(10, b)[:, 0:1], in1=r(11, b), op0=ALU.mult, op1=ALU.add)
                    if b < TB - 1:
                        last.then_inc(dve_step, t.dve_step.inc())
                        dve.wait_ge(dve_step, t.dve_step.now())
                last.then_inc(comb_ready, t.comb_ready.inc())
                dve.wait_ge(route_done, t.route_done.next())
                V.tensor_copy(comb_t[:, 0, :], ps[0:EXPERTS, 7, :]).then_inc(dve_step, t.dve_step.inc())
                dve.wait_ge(dve_step, t.dve_step.now())

            V.memset(w_raw[:], 0.0).then_inc(raw_zeroed, t.raw_zeroed.inc())
            dve.wait_ge(setup_landed, SETUP_LANDED)
            V.tensor_copy(trig[:, 3, :], pos_i[:]).then_inc(dve_step, t.dve_step.inc())
            dve.wait_ge(dve_step, t.dve_step.now())
            for n in range(2):
                ang, turns_n = trig[:, n, :], tmp[:, 0, :]
                V.tensor_scalar(ang, trig[:, 3, :], const[:, K_FREQ + n:K_FREQ + n + 1], None, ALU.mult).then_inc(dve_step, t.dve_step.inc())
                dve.wait_ge(dve_step, t.dve_step.now())
                V.tensor_scalar(turns_n, ang, 1.0 / TWO_PI, ROUND_MAGIC, ALU.mult, ALU.add).then_inc(dve_step, t.dve_step.inc())
                dve.wait_ge(dve_step, t.dve_step.now())
                V.tensor_scalar(turns_n, turns_n, ROUND_MAGIC, None, ALU.subtract).then_inc(dve_step, t.dve_step.inc())
                dve.wait_ge(dve_step, t.dve_step.now())
                for part in (PI_A, PI_B, PI_C):
                    V.scalar_tensor_tensor(out=ang, in0=turns_n, scalar=-part, in1=ang, op0=ALU.mult, op1=ALU.add).then_inc(dve_step, t.dve_step.inc())
                    dve.wait_ge(dve_step, t.dve_step.now())
                V.tensor_scalar(ang, ang, SIN_MAX, -SIN_MAX, ALU.min, ALU.max).then_inc(ang_ready, t.ang_ready.inc())
            V.tensor_copy(wr_hi[:], wr_raw[:]).then_inc(dve_step, t.dve_step.inc())
            dve.wait_ge(dve_step, t.dve_step.now())
            V.tensor_tensor(wr_lo[:], wr_raw[:], wr_hi[:].bitcast(F32), ALU.subtract).then_inc(wr_ready, t.wr_ready.inc())
            for k in range(KC):
                dve.wait_ge(x_turns, t.x_turns.next())
                V.tensor_copy(x[:, k, :], ps[:, k % 2, :]).then_inc(x_turned, t.x_turned.inc())
            dve.wait_ge(x_turned, t.x_turned.now())
            dve.wait_ge(act_step, t.act_step.now() + 4)
            t.act_step.add(4)

            for l in range(DEPTH):
                norm(x, KC, gains[:, 3 * l, :], h_hi, h_lo)
                V.memset(q_all[HD:HD + 1, :, :], 1.0).then_inc(qrow_ready, t.qrow_ready.inc())
                with turns(dve, 3, {t.unit_done: 2, t.q_ready: 1}) as j:
                    dve.wait_ge(unit_done, t.unit_done.next())
                    V.tensor_scalar(q_all[0:HD, j * 2, :], ps[0:HD, 0, :], HD**-0.5, None, ALU.mult)
                    V.tensor_scalar(q_all[0:HD, j * 2 + 1, :], ps[HD:P, 0, :], HD**-0.5, None, ALU.mult).then_inc(q_ready, t.q_ready.inc())
                    t.unit_done.add()
                v_blocks(3)
                dve.wait_ge(unit_done, t.unit_done.next())
                V.tensor_scalar(scan_t[:, 0, :], ps[0:FOX_HEADS, 5, :], b_forget[:, l:l + 1], None, ALU.add).then_inc(fz_taken, t.fz_taken.inc())
                dve.wait_ge(fz_taken, t.fz_taken.now())
                V.tensor_scalar(scan[:, 1, :], scan_t[:, 0, :], 0.0, None, ALU.min).then_inc(dve_step, t.dve_step.inc())
                dve.wait_ge(dve_step, t.dve_step.now())
                dve.wait_ge(fz_ready, t.fz_ready.next())
                V.tensor_tensor(scan[:, 0, :], scan_t[:, 3, :], scan[:, 1, :], ALU.subtract).then_inc(dve_step, t.dve_step.inc())
                dve.wait_ge(dve_step, t.dve_step.now())
                d, at_row = 1, 0
                while d < T:
                    src, dst = scan[:, at_row, :], scan[:, 1 - at_row, :]
                    V.tensor_copy(dst[:, 0:d], src[:, 0:d]).then_inc(dve_step, t.dve_step.inc())
                    dve.wait_ge(dve_step, t.dve_step.now())
                    add = V.tensor_tensor(dst[:, d:T], src[:, d:T], src[:, 0:T - d], ALU.add)
                    d, at_row = 2 * d, 1 - at_row
                    if d < T:
                        add.then_inc(dve_step, t.dve_step.inc())
                        dve.wait_ge(dve_step, t.dve_step.now())
                    else:
                        add.then_inc(negd_ready, t.negd_ready.inc())
                assert at_row == 1
                attention(3, 0, 0)
                V.memset(k_all[HD:HD + 1, :, :], 0.0).then_inc(qrow_ready, t.qrow_ready.inc())
                with turns(dve, 3, {t.unit_done: 2, t.raw_ready: 2, t.rot_done: 2, t.dve_step: 2, t.rope_ready: 2}) as j:
                    for s, dst in enumerate((q_all, k_all)):
                        t.unit_done.add()
                        rope(s, 2 + s, P, cos_d, sin_d, [(dst[0:HD, j * 2, :], 0, HD), (dst[0:HD, j * 2 + 1, :], HD, P)])
                v_blocks(3)
                attention(3, 3, 1)
                t.unit_done.add(5)
                rope(0, 5, QK_M, cos_m, sin_m, [(k_all[NOPE:QK_M, hd, :], NOPE, QK_M) for hd in range(MLA_HEADS)])
                norm(cq_raw, 2, gains_r[:, 2 * l, :], cn_hi, cn_lo)
                t.unit_done.add()
                for hd in range(MLA_HEADS):
                    rope(hd % 2, 5 + hd % 2, QK_M, cos_m, sin_m, [(q_all[0:QK_M, hd, :], 0, QK_M)])
                norm(ckv_raw, 2, gains_r[:, 2 * l + 1, :], cn_hi, cn_lo)
                t.unit_done.add()
                for hd in range(MLA_HEADS):
                    t.raw_ready.add()
                    dve.wait_ge(v_turns, t.v_turns.next())
                    V.tensor_copy(v_all[:, :, hd * HD:(hd + 1) * HD],
                                         ps[:, 4 + hd % 2, :].rearrange("p (b n) -> p b n", b=TB)[:, :, NOPE:P]).then_inc(v_ready, t.v_ready.inc())
                attention(2, 6, 0)
                with turns(dve, KC, {t.unit_done: 4, t.sig_ready: 3, t.dve_step: 2, t.m_ready: 1, t.mhi_ready: 1, t.mlo_ready: 1}) as m:
                    dve.wait_ge(unit_done, t.unit_done.next(4))
                    dve.wait_ge(sig_ready, t.sig_ready.next(3))
                    for b in range(3):
                        last = V.tensor_tensor(tmp[:, b, :], sg[:, b, :], ps[:, 3 + b, :], ALU.mult)
                    last.then_inc(dve_step, t.dve_step.inc())
                    dve.wait_ge(dve_step, t.dve_step.now())
                    V.tensor_tensor(tmp[:, 0, :], tmp[:, 0, :], tmp[:, 1, :], ALU.add).then_inc(dve_step, t.dve_step.inc())
                    dve.wait_ge(dve_step, t.dve_step.now())
                    V.tensor_tensor(tmp[:, 0, :], tmp[:, 0, :], tmp[:, 2, :], ALU.add).then_inc(m_ready, t.m_ready.inc())
                    dve.wait_ge(mhi_ready, t.mhi_ready.next())
                    dve.wait_ge(m_ready, t.m_ready.now())
                    V.tensor_tensor(m_lo[:, m, :], tmp[:, 0, :], m_hi[:, m, :].bitcast(F32), ALU.subtract).then_inc(mlo_ready, t.mlo_ready.inc())
                with turns(dve, KC // 2, {t.unit_done: 2, t.x_upd: 2}) as m:
                    for s in range(2):
                        dve.wait_ge(unit_done, t.unit_done.next())
                        V.tensor_tensor(x[:, m * 2 + s, :], x[:, m * 2 + s, :], ps[:, 6 + s, :], ALU.add).then_inc(x_upd, t.x_upd.inc())
                dve.wait_ge(x_upd, t.x_upd.now())
                norm(x, KC, gains[:, 3 * l + 1, :], h_hi, h_lo)
                for c in range(PLE // P):
                    dve.wait_ge(phi_ready, t.phi_ready.next())
                    V.tensor_tensor(p_lo[:, c, :], ps[:, 4 + c, :], p_hi[:, c, :].bitcast(F32), ALU.subtract).then_inc(plo_ready, t.plo_ready.inc())

                def expert(e):
                    sparse = e is not None
                    if sparse:
                        V.tensor_scalar(comb_t[:, 1, :], comb_t[:, 0, :], ident[0:EXPERTS, bass.ds(e, 1)], None, ALU.mult).then_inc(comb_ready, t.comb_ready.inc())
                    with turns(dve, FB, {t.unit_done: 2, t.sig_ready: 1, t.af_ready: 1, t.ahi_ready: 1, t.alo_ready: 1}) as f:
                        dve.wait_ge(unit_done, t.unit_done.next(2))
                        dve.wait_ge(sig_ready, t.sig_ready.next())
                        V.tensor_tensor(tmp[:, 0, :], sg[:, 0, :], ps[:, 1, :], ALU.mult).then_inc(af_ready, t.af_ready.inc())
                        dve.wait_ge(ahi_ready, t.ahi_ready.next())
                        dve.wait_ge(af_ready, t.af_ready.now())
                        V.tensor_tensor(a_lo[:, f, :], tmp[:, 0, :], a_hi[:, f, :].bitcast(F32), ALU.subtract).then_inc(alo_ready, t.alo_ready.inc())
                    if sparse:
                        dve.wait_ge(route_done, t.route_done.next())
                        V.tensor_copy(comb_b[:], ps[:, 4, :])
                        V.memset(gate[:, 2:3], 0.0).then_inc(dve_step, t.dve_step.inc())
                    with turns(dve, KC // 2, {t.unit_done: 2, t.x_upd: 2} | ({t.dve_step: 2} if sparse else {})) as m:
                        for s in range(2):
                            dve.wait_ge(unit_done, t.unit_done.next())
                            xm, y = x[:, m * 2 + s, :], ps[:, 2 + s, :]
                            if sparse:
                                dve.wait_ge(dve_step, t.dve_step.now())
                                dve.wait_ge(x_upd, t.x_upd.now(back=1))
                                V.tensor_tensor(tmp[:, 2 + s, :], y, comb_b[:], ALU.mult).then_inc(dve_step, t.dve_step.inc())
                                dve.wait_ge(dve_step, t.dve_step.now())
                                y = tmp[:, 2 + s, :]
                            V.tensor_tensor(xm, xm, y, ALU.add).then_inc(x_upd, t.x_upd.inc())
                    dve.wait_ge(x_upd, t.x_upd.now())

                expert_per = {t.unit_done: EXPERT_UNITS, t.sig_ready: FB, t.af_ready: FB, t.ahi_ready: FB, t.alo_ready: FB, t.x_upd: KC}
                if l % 2 == 0:
                    with turns(dve, 2, expert_per):
                        expert(None)
                else:
                    dve.wait_ge(route_done, t.route_done.next())
                    routing()
                    with turns(dve, EXPERTS, expert_per | {t.comb_ready: 1, t.route_done: 1, t.dve_step: 1 + KC}) as e:
                        expert(e)
                t.unit_done.add(2)
                norm(x, KC, gains[:, 3 * l + 2, :], h_hi, h_lo)
                dve.wait_ge(pp_ready, t.pp_ready.next(KC))
                with turns(dve, KC // 2, {t.unit_done: 2, t.sig_ready: 2, t.dve_step: 2, t.x_upd: 2}) as m:
                    for s in range(2):
                        t.unit_done.add()
                        dve.wait_ge(sig_ready, t.sig_ready.next())
                        V.tensor_tensor(tmp[:, s, :], sg[:, s, :], pp[:, m * 2 + s, :], ALU.mult).then_inc(dve_step, t.dve_step.inc())
                        dve.wait_ge(dve_step, t.dve_step.now())
                        V.tensor_tensor(x[:, m * 2 + s, :], x[:, m * 2 + s, :], tmp[:, s, :], ALU.add).then_inc(x_upd, t.x_upd.inc())
                dve.wait_ge(x_upd, t.x_upd.now())
            dve.wait_ge(root_ready, t.root_ready.next())
            V.reciprocal(rstd[:], rstd[:]).then_inc(dve_step, t.dve_step.inc())
            dve.wait_ge(dve_step, t.dve_step.now())
            for k in range(KC):
                V.scalar_tensor_tensor(out=x[:, k, :], in0=x[:, k, :], scalar=gains[:, 3 * DEPTH, k:k + 1],
                                              in1=rstd[:], op0=ALU.mult, op1=ALU.mult).then_inc(xn_ready, t.xn_ready.inc())
            for b in range(TB):
                for half in range(2):
                    dve.wait_ge(out_turns, t.out_turns.next())
                    V.tensor_copy(x_tok[:, b, half * T:(half + 1) * T], ps[:, half, :]).then_inc(out_ready, t.out_ready.inc())


_INS = ["x", "p", "positions", "mix_norm", "w_in", "b_forget", "mla_q_norm", "mla_kv_norm", "w_uq", "w_ukv",
        "w_br_fox", "w_br_dil", "w_br_mla", "w_out", "ffn_norm", "w_ffn_gate", "w_ffn_up", "w_ffn_down",
        "w_router", "w_exp_gate", "w_exp_up", "w_exp_down", "ple_norm", "w_ple_gate", "w_ple_proj", "final_norm"]


def kernel(**inputs):
    import numpy as _np
    import concourse.bacc as _bacc
    from concourse import mybir as _mybir
    from concourse.bass_utils import run_bass_kernel_spmd as _run

    nc = _bacc.Bacc("TRN2", target_bir_lowering=False, num_devices=1)
    arrays, aps = {}, {}
    tables = {"const": constant_table()}
    for name in _INS + ["const"]:
        array = _np.ascontiguousarray(tables[name] if name in tables else inputs[name])
        arrays[f"in_{name}_dram"] = array
        aps[name] = nc.dram_tensor(f"in_{name}_dram", array.shape, _mybir.dt.from_np(array.dtype), kind="ExternalInput").ap()
    out = nc.dram_tensor("out_0_dram", (1, T, D), _mybir.dt.float32, kind="ExternalOutput").ap()
    build_trunk(nc, aps, out)
    r = _run(nc, [arrays], core_ids=[0])
    return r.results[0]["out_0_dram"]
```

```python
from contextlib import ExitStack, contextmanager

import numpy as np

import concourse.bass as bass
from concourse import mybir

F32 = mybir.dt.float32
F32R = mybir.dt.float32r
I32 = mybir.dt.int32
U32 = mybir.dt.uint32
ALU = mybir.AluOpType
ACT = mybir.ActivationFunctionType

P = 128
D = 1024
T = 512
DEPTH = 2
HD = 64
KC = D // P
TB = T // P
FOX_HEADS = DIL_HEADS = 6
MLA_HEADS = 4
NOPE, ROPE_M = 64, 32
QK_M = NOPE + ROPE_M
WIDTH = FOX_HEADS * HD
RANK = 256
PLE = 256
EXPERTS = 8
F_EXP = 1408
FB = F_EXP // P
UNIT_CHUNKS = FB
UNIT = UNIT_CHUNKS * P
EPS = 1e-6
THETA = 10000.0
MASKED = -1e30
CAP = 160
ROUNDS = -(-T // CAP)
RING = 6
SLOT_TILES = ((0, 0), (CAP - P, 2 * P - CAP))
CREDIT = 4

C_FQ, C_FK, C_FV = 0, WIDTH, 2 * WIDTH
C_FZ = 3 * WIDTH
C_DQ = C_FZ + FOX_HEADS
C_DK, C_DV = C_DQ + WIDTH, C_DQ + 2 * WIDTH
C_CQ = C_DQ + 3 * WIDTH
C_CKV = C_CQ + RANK
C_KR = C_CKV + RANK
C_GATES = C_KR + ROPE_M

K_IDENT, K_ONES, K_ROTD, K_ROTM = 0, P, 2 * P, 3 * P
K_BIAS = 4 * P
K_FREQ = K_BIAS + 2 * T
K_EPS, K_HALFPI = K_FREQ + 2, K_FREQ + 3
K_IOTA = K_FREQ + 4
K_BEFORE = K_IOTA + EXPERTS
K_SLOTS = K_BEFORE + P
K_COLS = K_SLOTS + CAP

EXPERT_UNITS = 2 * FB + KC
SETUP_LANDED = 16 * (5 * DEPTH + 2)

TWO_PI = 2 * np.pi
PI_A = 6.28125
PI_B = float(np.float32(np.round((TWO_PI - PI_A) * 2**21) / 2**21))
PI_C = float(np.float32(TWO_PI - PI_A - PI_B))
SIN_MAX = 3.1415925
ROUND_MAGIC = 1.5 * 2.0**23
DIL_PAIRS = ((128, 1), (512, 4), (2048, 16))


def constant_table():
    c = np.zeros((P, K_COLS), np.float32)
    c[:, K_IDENT:K_IDENT + P] = np.eye(P)
    c[:, K_ONES:K_ONES + P] = 1.0
    for base, width, half in ((0, HD, HD // 2), (HD, HD, HD // 2)):
        for i in range(half):
            c[base + i + half, K_ROTD + base + i] = -1.0
            c[base + i, K_ROTD + base + i + half] = 1.0
    for i in range(ROPE_M // 2):
        c[NOPE + i + ROPE_M // 2, K_ROTM + NOPE + i] = -1.0
        c[NOPE + i, K_ROTM + NOPE + i + ROPE_M // 2] = 1.0
    q = np.arange(P)[:, None]
    dist = q + (TB - 1) * P - np.arange(T)[None, :]
    c[:, K_BIAS:K_BIAS + T] = np.where(dist >= 0, 0.0, MASKED)
    times = sum(((dist >= 0) & (dist % r == 0) & (dist <= w)).astype(np.float64) for w, r in DIL_PAIRS)
    c[:, K_BIAS + T:K_BIAS + 2 * T] = np.where(times > 0, np.log(np.maximum(times, 1)), MASKED)
    half = HD // 2
    f = THETA ** (-(np.arange(half, dtype=np.float32) / half).astype(np.float64))
    c[:, K_FREQ] = np.tile(f, P // half)
    half = ROPE_M // 2
    f = THETA ** (-(np.arange(half, dtype=np.float32) / half).astype(np.float64))
    c[NOPE:NOPE + ROPE_M, K_FREQ + 1] = np.tile(f, 2)
    c[:, K_EPS] = EPS
    c[:, K_HALFPI] = np.pi / 2
    c[:, K_IOTA:K_IOTA + EXPERTS] = np.arange(EXPERTS)
    c[:, K_BEFORE:K_BEFORE + P] = np.arange(P)[:, None] < np.arange(P)[None, :]
    c[:, K_SLOTS:K_SLOTS + CAP] = np.arange(CAP)
    return c


class Tally:

    def __init__(self, sem, start=CREDIT):
        self.sem, self.base, self.k = sem, start, 0

    def add(self, n=1):
        self.k += n

    def inc(self):
        self.k += 1
        return 1

    def next(self, n=1):
        self.k += n
        return self.base + self.k

    def now(self, back=0):
        return self.base + (self.k - back)


class Tallies:

    def __init__(self, s):
        self.w_landed0 = Tally(s["w_landed0"], 0)
        self.w_landed1 = Tally(s["w_landed1"], 0)
        self.table_landed = Tally(s["table_landed"], 0)
        self.setup_landed = Tally(s["setup_landed"], 0)
        self.x_landed = Tally(s["x_landed"], 0)
        self.p_landed = Tally(s["p_landed"], 0)
        self.negd_landed = Tally(s["negd_landed"], 0)
        self.out_landed = Tally(s["out_landed"], 0)
        self.unit_done = Tally(s["unit_done"])
        self.x_turns = Tally(s["x_turns"])
        self.v_turns = Tally(s["v_turns"])
        self.p_turns = Tally(s["p_turns"])
        self.out_turns = Tally(s["out_turns"])
        self.norm_mm = Tally(s["norm_mm"])
        self.rot_done = Tally(s["rot_done"])
        self.s_done = Tally(s["s_done"])
        self.t_done = Tally(s["t_done"])
        self.pv_done = Tally(s["pv_done"])
        self.route_done = Tally(s["route_done"])
        self.rank_done = Tally(s["rank_done"])
        self.htok_turned = Tally(s["htok_turned"])
        self.gathered = Tally(s["gathered"])
        self.sel_turned = Tally(s["sel_turned"])
        self.cw_done = Tally(s["cw_done"])
        self.y_turned = Tally(s["y_turned"])
        self.scattered = Tally(s["scattered"])
        self.hthi_ready = Tally(s["hthi_ready"])
        self.hgeven_ready = Tally(s["hgeven_ready"])
        self.yhi_ready = Tally(s["yhi_ready"])
        self.hi_done = Tally(s["hi_done"])
        self.act_step = Tally(s["act_step"])
        self.sq_ready = Tally(s["sq_ready"])
        self.root_ready = Tally(s["root_ready"])
        self.hn_ready = Tally(s["hn_ready"])
        self.raw_ready = Tally(s["raw_ready"])
        self.k_ready = Tally(s["k_ready"])
        self.sig_ready = Tally(s["sig_ready"])
        self.mhi_ready = Tally(s["mhi_ready"])
        self.ahi_ready = Tally(s["ahi_ready"])
        self.exp_done = Tally(s["exp_done"])
        self.pt_even = Tally(s["pt_even"])
        self.ohi_ready = Tally(s["ohi_ready"])
        self.fz_ready = Tally(s["fz_ready"])
        self.phi_ready = Tally(s["phi_ready"])
        self.pp_ready = Tally(s["pp_ready"])
        self.share_ready = Tally(s["share_ready"])
        self.dve_step = Tally(s["dve_step"])
        self.raw_zeroed = Tally(s["raw_zeroed"])
        self.x_turned = Tally(s["x_turned"])
        self.ang_ready = Tally(s["ang_ready"])
        self.hf_ready = Tally(s["hf_ready"])
        self.sum_ready = Tally(s["sum_ready"])
        self.hlo_ready = Tally(s["hlo_ready"])
        self.q_ready = Tally(s["q_ready"])
        self.rope_ready = Tally(s["rope_ready"])
        self.v_ready = Tally(s["v_ready"])
        self.fz_taken = Tally(s["fz_taken"])
        self.negd_ready = Tally(s["negd_ready"])
        self.s_taken = Tally(s["s_taken"])
        self.neg_ready = Tally(s["neg_ready"])
        self.p_ready = Tally(s["p_ready"])
        self.pt_odd = Tally(s["pt_odd"])
        self.olo_ready = Tally(s["olo_ready"])
        self.m_ready = Tally(s["m_ready"])
        self.mlo_ready = Tally(s["mlo_ready"])
        self.x_upd = Tally(s["x_upd"])
        self.af_ready = Tally(s["af_ready"])
        self.alo_ready = Tally(s["alo_ready"])
        self.plo_ready = Tally(s["plo_ready"])
        self.out_ready = Tally(s["out_ready"])
        self.xn_ready = Tally(s["xn_ready"])
        self.comb_ready = Tally(s["comb_ready"])
        self.logits_taken = Tally(s["logits_taken"])
        self.qrow_ready = Tally(s["qrow_ready"])
        self.gap_ready = Tally(s["gap_ready"])
        self.mask_ready = Tally(s["mask_ready"])
        self.tops_ready = Tally(s["tops_ready"])
        self.htlo_ready = Tally(s["htlo_ready"])
        self.sel_ready = Tally(s["sel_ready"])
        self.hgodd_ready = Tally(s["hgodd_ready"])
        self.selt_ready = Tally(s["selt_ready"])
        self.cw_ready = Tally(s["cw_ready"])
        self.y_taken = Tally(s["y_taken"])
        self.y32_ready = Tally(s["y32_ready"])
        self.ylo_ready = Tally(s["ylo_ready"])
        self.moe_step = Tally(s["moe_step"])
        self.e_landed0 = Tally(s["e_landed0"], 0)
        self.e_landed1 = Tally(s["e_landed1"], 0)
        self.e_landed2 = Tally(s["e_landed2"], 0)
        self.e_landed3 = Tally(s["e_landed3"], 0)
        self.e_landed4 = Tally(s["e_landed4"], 0)
        self.e_landed5 = Tally(s["e_landed5"], 0)
        self.expert_unit_done = Tally(s["expert_unit_done"], RING)
        self.silu_ready = Tally(s["silu_ready"])
        self.expert_act_ready = Tally(s["expert_act_ready"])
        self.tokens_added = Tally(s["tokens_added"])
        self.moe_done = Tally(s["moe_done"])
        self.lo_done = Tally(s["lo_done"])
        self.q_staged = Tally(s["q_staged"])
        self.v_staged = Tally(s["v_staged"])


@contextmanager
def turns(eng, count, per):
    with eng.Fori(0, count) as i:
        saved = {t: (t.base, t.k) for t in per}
        for t, n in per.items():
            t.base, t.k = t.now() + i * n, 0
        yield i
        for t, n in per.items():
            assert t.k == n, (t.sem, t.k, n)
    for t, n in per.items():
        t.base, t.k = saved[t][0], saved[t][1] + count * n


def build_trunk(nc, a, out):
    with ExitStack() as ctx:
        def sb(name, shape, dt=F32):
            return ctx.enter_context(nc.sbuf_tensor(name, shape, dt))

        x = sb("x", [P, KC, T])
        h_hi, h_lo = sb("h_hi", [P, KC, T], F32R), sb("h_lo", [P, KC, T], F32R)
        w_raw = sb("w_raw", [P, 2, UNIT])
        w_hi, w_lo = sb("w_hi", [P, 2, UNIT], F32R), sb("w_lo", [P, 2, UNIT], F32R)
        def slab(name, nbytes):
            start = -(-nc.sbuf_base // 32) * 32
            sb(name, [P, nbytes // 4 + 8])
            assert start + nbytes <= nc.sbuf_base
            return start

        at0, at1, at2 = slab("slab0", 65536), slab("slab1", 16384), slab("slab2", 9216)
        const = sb("const", [P, K_COLS])
        gains = sb("gains", [P, 3 * DEPTH + 1, KC])
        gains_r = sb("gains_r", [P, 2 * DEPTH, RANK // P])
        b_forget = sb("b_forget", [FOX_HEADS, DEPTH])
        cos_d, sin_d = sb("cos_d", [P, T]), sb("sin_d", [P, T])
        cos_m, sin_m = sb("cos_m", [P, T]), sb("sin_m", [P, T])
        tmp = sb("tmp", [P, 4, T])
        sq = sb("sq", [P, 2, T])
        rstd = sb("rstd", [P, T])
        v_st = sb("v_st", [P, 2, TB, HD])
        smax, sneg = sb("smax", [P, 2, TB]), sb("sneg", [P, 2, TB])
        ssum, srec = sb("ssum", [P, 2, TB]), sb("srec", [P, 2, TB])
        gate = sb("gate", [P, 14])
        route = sb("route", [P, 12, TB, EXPERTS])
        route_i = sb("route_i", [P, TB, EXPERTS], U32)
        tops = sb("tops", [1, ROUNDS], I32)
        comb_tab, rank_tab = sb("comb_tab", [P, TB, EXPERTS + 1]), sb("rank_tab", [P, TB, EXPERTS + 1])
        comb_e, rank_e = sb("comb_e", [P, TB, 1]), sb("rank_e", [P, TB, 1])
        slot_w = sb("slot_w", [P, 2])

        def at(name, shape, dt, offset):
            return nc.alloc_sbuf_tensor_at(name, shape, dt, offset=offset)

        pt = at("pt", [P, 10 * P], F32, at2)
        q_st = at("q_st", [P, 2, T], F32, at2 + 5120)
        o_hi = at("o_hi", [P, KC, T], F32R, at0)
        o_lo = at("o_lo", [P, KC, T], F32R, at0 + 16384)
        q_all = at("q_all", [P, FOX_HEADS, T], F32, at0 + 32768)
        k_all = at("k_all", [P, FOX_HEADS, T], F32, at0 + 45056)
        v_all = at("v_all", [P, TB, WIDTH], F32, at0 + 57344)
        probs = at("probs", [P, 2, TB, T], F32, at1)
        scan = at("scan", [FOX_HEADS, 2, T], F32, at1)
        scan_t = at("scan_t", [FOX_HEADS, 4, T], F32, at1 + 4096)
        cq_raw = at("cq_raw", [P, 2, T], F32, at1)
        cn_hi = at("cn_hi", [P, 2, T], F32R, at1 + 4096)
        cn_lo = at("cn_lo", [P, 2, T], F32R, at1 + 8192)
        ckv_raw = at("ckv_raw", [P, 2, T], F32, at1 + 12288)
        m_hi = at("m_hi", [P, KC, T], F32R, at0 + 32768)
        m_lo = at("m_lo", [P, KC, T], F32R, at0 + 49152)
        sg = at("sg", [P, 3, T], F32, at1)
        a_hi = at("a_hi", [P, FB, T], F32R, at0)
        a_lo = at("a_lo", [P, FB, T], F32R, at0 + 22528)
        p_hi = at("p_hi", [P, PLE // P, T], F32R, at0 + 45056)
        p_lo = at("p_lo", [P, PLE // P, T], F32R, at0 + 49152)
        p_tok = at("p_tok", [P, TB, PLE], F32, at1 + 8192)
        pp = at("pp", [P, KC, T], F32, at0)
        ga = at("ga", [P, FB, CAP], F32, at0)
        y_hi = at("y_hi", [P, 2, D], F32R, at2)
        hg = at("hg", [P, KC, CAP], F32, at0 + 8448)
        y_t = at("y_t", [P, KC, CAP], F32, at0 + 8448)
        ring_a = at("ring_a", [P, RING - 1, UNIT], F32, at0 + 14592)
        ring_b = at("ring_b", [P, UNIT], F32, at0 + 53248)
        sel = at("sel", [P, TB, CAP], F32R, at0 + 58880)
        silu = at("silu", [P, 3, CAP], F32, at1)
        sel_t = at("sel_t", [P, 2, T], F32R, at1 + 4096)
        y_lo = at("y_lo", [P, 2, D], F32R, at1 + 8192)
        ring = [ring_a[:, s, :] for s in range(RING - 1)] + [ring_b[:]]
        x_tok = at("x_tok", [P, TB, D], F32, at1)
        pos_i = at("pos_i", [P, T], I32, at0)
        trig = at("trig", [P, 4, T], F32, at0 + 2048)

        ident = const[:, K_IDENT:K_IDENT + P]
        ones = const[:, K_ONES:K_ONES + P]
        rot_d = const[:, K_ROTD:K_ROTD + P]
        rot_m = const[0:QK_M, K_ROTM:K_ROTM + QK_M]

        ps = ctx.enter_context(nc.psum_tensor("ps", [P, 8, T], F32))

        def sem(name):
            return ctx.enter_context(nc.semaphore(name))

        w_landed0 = sem("w_landed0")
        w_landed1 = sem("w_landed1")
        e_landed0 = sem("e_landed0")
        e_landed1 = sem("e_landed1")
        e_landed2 = sem("e_landed2")
        e_landed3 = sem("e_landed3")
        e_landed4 = sem("e_landed4")
        e_landed5 = sem("e_landed5")
        table_landed = sem("table_landed")
        setup_landed = sem("setup_landed")
        x_landed = sem("x_landed")
        p_landed = sem("p_landed")
        negd_landed = sem("negd_landed")
        out_landed = sem("out_landed")
        unit_done = sem("unit_done")
        x_turns = sem("x_turns")
        v_turns = sem("v_turns")
        p_turns = sem("p_turns")
        out_turns = sem("out_turns")
        norm_mm = sem("norm_mm")
        rot_done = sem("rot_done")
        s_done = sem("s_done")
        t_done = sem("t_done")
        pv_done = sem("pv_done")
        route_done = sem("route_done")
        rank_done = sem("rank_done")
        htok_turned = sem("htok_turned")
        gathered = sem("gathered")
        sel_turned = sem("sel_turned")
        cw_done = sem("cw_done")
        y_turned = sem("y_turned")
        scattered = sem("scattered")
        expert_unit_done = sem("expert_unit_done")
        hthi_ready = sem("hthi_ready")
        hgeven_ready = sem("hgeven_ready")
        yhi_ready = sem("yhi_ready")
        silu_ready = sem("silu_ready")
        hi_done = sem("hi_done")
        act_step = sem("act_step")
        sq_ready = sem("sq_ready")
        root_ready = sem("root_ready")
        hn_ready = sem("hn_ready")
        raw_ready = sem("raw_ready")
        k_ready = sem("k_ready")
        sig_ready = sem("sig_ready")
        mhi_ready = sem("mhi_ready")
        ahi_ready = sem("ahi_ready")
        exp_done = sem("exp_done")
        pt_even = sem("pt_even")
        ohi_ready = sem("ohi_ready")
        fz_ready = sem("fz_ready")
        phi_ready = sem("phi_ready")
        pp_ready = sem("pp_ready")
        share_ready = sem("share_ready")
        dve_step = sem("dve_step")
        raw_zeroed = sem("raw_zeroed")
        x_turned = sem("x_turned")
        ang_ready = sem("ang_ready")
        hf_ready = sem("hf_ready")
        sum_ready = sem("sum_ready")
        hlo_ready = sem("hlo_ready")
        q_ready = sem("q_ready")
        rope_ready = sem("rope_ready")
        v_ready = sem("v_ready")
        fz_taken = sem("fz_taken")
        negd_ready = sem("negd_ready")
        s_taken = sem("s_taken")
        neg_ready = sem("neg_ready")
        p_ready = sem("p_ready")
        pt_odd = sem("pt_odd")
        olo_ready = sem("olo_ready")
        m_ready = sem("m_ready")
        mlo_ready = sem("mlo_ready")
        x_upd = sem("x_upd")
        af_ready = sem("af_ready")
        alo_ready = sem("alo_ready")
        plo_ready = sem("plo_ready")
        out_ready = sem("out_ready")
        xn_ready = sem("xn_ready")
        comb_ready = sem("comb_ready")
        logits_taken = sem("logits_taken")
        qrow_ready = sem("qrow_ready")
        gap_ready = sem("gap_ready")
        mask_ready = sem("mask_ready")
        tops_ready = sem("tops_ready")
        htlo_ready = sem("htlo_ready")
        sel_ready = sem("sel_ready")
        hgodd_ready = sem("hgodd_ready")
        selt_ready = sem("selt_ready")
        cw_ready = sem("cw_ready")
        y_taken = sem("y_taken")
        y32_ready = sem("y32_ready")
        ylo_ready = sem("ylo_ready")
        moe_step = sem("moe_step")
        expert_act_ready = sem("expert_act_ready")
        tokens_added = sem("tokens_added")
        moe_done = sem("moe_done")
        lo_done = sem("lo_done")
        q_staged = sem("q_staged")
        v_staged = sem("v_staged")
        sems = dict(
            w_landed0=w_landed0, w_landed1=w_landed1, setup_landed=setup_landed, table_landed=table_landed, x_landed=x_landed,
            p_landed=p_landed, negd_landed=negd_landed, out_landed=out_landed, unit_done=unit_done,
            x_turns=x_turns, v_turns=v_turns, p_turns=p_turns, out_turns=out_turns, norm_mm=norm_mm,
            rot_done=rot_done, s_done=s_done, t_done=t_done, pv_done=pv_done, route_done=route_done,
            rank_done=rank_done, htok_turned=htok_turned, gathered=gathered, sel_turned=sel_turned,
            cw_done=cw_done, y_turned=y_turned, scattered=scattered, hthi_ready=hthi_ready,
            hgeven_ready=hgeven_ready, yhi_ready=yhi_ready, hi_done=hi_done, act_step=act_step,
            sq_ready=sq_ready, root_ready=root_ready, hn_ready=hn_ready, raw_ready=raw_ready,
            k_ready=k_ready, sig_ready=sig_ready, mhi_ready=mhi_ready, ahi_ready=ahi_ready,
            exp_done=exp_done, pt_even=pt_even, ohi_ready=ohi_ready, fz_ready=fz_ready,
            phi_ready=phi_ready, pp_ready=pp_ready, share_ready=share_ready, dve_step=dve_step,
            raw_zeroed=raw_zeroed, x_turned=x_turned, ang_ready=ang_ready, hf_ready=hf_ready,
            hlo_ready=hlo_ready, q_ready=q_ready, rope_ready=rope_ready, v_ready=v_ready,
            fz_taken=fz_taken, negd_ready=negd_ready, s_taken=s_taken, neg_ready=neg_ready,
            p_ready=p_ready, pt_odd=pt_odd, olo_ready=olo_ready, m_ready=m_ready,
            mlo_ready=mlo_ready, x_upd=x_upd, af_ready=af_ready, alo_ready=alo_ready,
            plo_ready=plo_ready, out_ready=out_ready, xn_ready=xn_ready, comb_ready=comb_ready,
            logits_taken=logits_taken, qrow_ready=qrow_ready, gap_ready=gap_ready, mask_ready=mask_ready,
            tops_ready=tops_ready, htlo_ready=htlo_ready, sel_ready=sel_ready,
            hgodd_ready=hgodd_ready, selt_ready=selt_ready, cw_ready=cw_ready, y_taken=y_taken,
            y32_ready=y32_ready, ylo_ready=ylo_ready, moe_step=moe_step, lo_done=lo_done,
            sum_ready=sum_ready, q_staged=q_staged, v_staged=v_staged, e_landed0=e_landed0, e_landed1=e_landed1, e_landed2=e_landed2,
            e_landed3=e_landed3, e_landed4=e_landed4, e_landed5=e_landed5,
            expert_unit_done=expert_unit_done, silu_ready=silu_ready,
            expert_act_ready=expert_act_ready, tokens_added=tokens_added, moe_done=moe_done)

        def rows(w, chunks):
            return w.rearrange("(c p) n -> p c n", c=chunks)

        block = ctx.enter_context(nc.Block())

        @block.sync
        def _(sp):
            t = Tallies(sems)
            loads = Tally(lo_done)
            landed = [t.w_landed0, t.w_landed1]
            slot = [0]

            def load(src, chunks, width):
                s = slot[0]
                sp.wait_ge(lo_done, loads.now(back=1))
                dst = w_raw[:, s, 0:chunks * width].rearrange("p (c n) -> p c n", c=chunks)
                sp.dma_start(dst, src).then_inc(landed[s].sem, 16)
                loads.add()
                slot[0] = 1 - s

            e_loads = Tally(expert_unit_done, RING)
            e_landed = [t.e_landed0, t.e_landed1, t.e_landed2, t.e_landed3, t.e_landed4, t.e_landed5]

            def load_expert(s, src, chunks, free=1):
                if free:
                    sp.wait_ge(expert_unit_done, e_loads.now(back=RING - free))
                sp.dma_start(ring[s][:, 0:chunks * P].rearrange("p (c n) -> p c n", c=chunks), src).then_inc(e_landed[s].sem, 16)
                e_loads.add()

            def cols(w, chunks, c0, width=P):
                start = c0 if isinstance(c0, int) else sp.snap(c0)
                return rows(w, chunks)[:, :, bass.ds(start, width)]

            sp.dma_start(pos_i[:], a["positions"].to_broadcast([P, T])).then_inc(table_landed, 16)
            sp.dma_start(const[:], a["const"]).then_inc(table_landed, 16)
            sp.dma_start(x_tok[:], a["x"][0].rearrange("(b p) d -> p b d", p=P)).then_inc(x_landed, 16)
            with nc.allow_non_contiguous_dma(reason="small gain vectors"):
                for l in range(DEPTH):
                    for n, name in enumerate(("mix_norm", "ffn_norm", "ple_norm")):
                        sp.dma_start(gains[:, 3 * l + n, :], a[name][l].rearrange("(c p) -> p c", p=P)).then_inc(setup_landed, 16)
                    for n, name in enumerate(("mla_q_norm", "mla_kv_norm")):
                        sp.dma_start(gains_r[:, 2 * l + n, :], a[name][l].rearrange("(c p) -> p c", p=P)).then_inc(setup_landed, 16)
                sp.dma_start(gains[:, 3 * DEPTH, :], a["final_norm"].rearrange("(c p) -> p c", p=P)).then_inc(setup_landed, 16)
                sp.dma_start(b_forget[:], a["b_forget"].rearrange("l h -> h l")).then_inc(setup_landed, 16)

            sp.wait_ge(raw_zeroed, t.raw_zeroed.next())
            for l in range(DEPTH):
                w_in = a["w_in"][l]
                with turns(sp, 3, {loads: 2}) as j:
                    load(cols(w_in, KC, C_FQ + j * P), KC, P)
                    load(cols(w_in, KC, C_FK + j * P), KC, P)
                load(cols(w_in, KC, C_FZ), KC, P)
                for j in range(3):
                    load(cols(w_in, KC, C_FV + j * P), KC, P)
                with turns(sp, 3, {loads: 2}) as j:
                    load(cols(w_in, KC, C_DQ + j * P), KC, P)
                    load(cols(w_in, KC, C_DK + j * P), KC, P)
                for j in range(3):
                    load(cols(w_in, KC, C_DV + j * P), KC, P)
                for c in (C_CQ, C_CQ + P, C_CKV, C_CKV + P, C_KR - NOPE):
                    load(cols(w_in, KC, c), KC, P)
                load(rows(a["w_uq"][l], 2), 2, MLA_HEADS * QK_M)
                load(rows(a["w_ukv"][l], 2), 2, MLA_HEADS * P)
                with turns(sp, KC, {loads: 4}) as m:
                    for b in range(3):
                        load(cols(w_in, KC, C_GATES + b * D + m * P), KC, P)
                    s = slot[0]
                    branches = [(n, rows(a[name][l], n)[:, :, bass.ds(m * (P // 2) * 2, P)]) for name, n in (("w_br_fox", 3), ("w_br_dil", 3), ("w_br_mla", 2))]
                    sp.wait_ge(lo_done, loads.now(back=1))
                    at_chunk = 0
                    for n, src in branches:
                        dst = w_raw[:, s, at_chunk * P:(at_chunk + n) * P].rearrange("p (c n) -> p c n", c=n)
                        sp.dma_start(dst, src).then_inc(landed[s].sem, 16)
                        at_chunk += n
                    loads.add()
                    slot[0] = 1 - s
                with turns(sp, KC // 2, {loads: 2}) as m:
                    for s in range(2):
                        load(cols(a["w_out"][l], KC, m * 2 * P + s * P), KC, P)
                sp.dma_start(p_tok[:], a["p"][l, 0].rearrange("(b p) d -> p b d", p=P)).then_inc(p_landed, 16)

                def expert(gate_w, up_w, down_w, col0=0):
                    with turns(sp, FB, {loads: 2}) as f:
                        load(cols(gate_w, KC, col0 + f * P), KC, P)
                        load(cols(up_w, KC, col0 + f * P), KC, P)
                    with turns(sp, KC // 2, {loads: 2}) as m:
                        for s in range(2):
                            load(cols(down_w, FB, m * 2 * P + s * P), FB, P)

                if l % 2 == 0:
                    for half in range(2):
                        expert(a["w_ffn_gate"][l // 2], a["w_ffn_up"][l // 2],
                               a["w_ffn_down"][l // 2][half * F_EXP:(half + 1) * F_EXP, :], half * F_EXP)
                if l % 2:
                    with nc.allow_non_contiguous_dma(reason="narrow matrix"):
                        load(rows(a["w_router"][l // 2], KC), KC, EXPERTS)
                for half in range(2):
                    load(cols(a["w_ple_proj"][l], 2, half * 4 * P, 4 * P), 2, 4 * P)
                if l % 2:
                    sp.wait_ge(tops_ready, t.tops_ready.next())
                    with turns(sp, ROUNDS, {e_loads: EXPERTS * EXPERT_UNITS}) as r:
                        with sp.If(sp.value_load(tops[0:1, bass.ds(r, 1)]) > 0):
                            with turns(sp, EXPERTS, {e_loads: EXPERT_UNITS}) as e:
                                pick = lambda w: w[l // 2, bass.ds(e, 1)].rearrange("o k n -> (o k) n")
                                gate_w, up_w, down_w = pick(a["w_exp_gate"]), pick(a["w_exp_up"]), pick(a["w_exp_down"])
                                with turns(sp, FB // 3, {e_loads: RING}) as f:
                                    for n in range(3):
                                        load_expert(2 * n, cols(gate_w, KC, f * (3 * P) + n * P), KC)
                                        load_expert(2 * n + 1, cols(up_w, KC, f * (3 * P) + n * P), KC)
                                for n in range(FB % 3):
                                    load_expert(2 * n, cols(gate_w, KC, (FB - FB % 3 + n) * P), KC)
                                    load_expert(2 * n + 1, cols(up_w, KC, (FB - FB % 3 + n) * P), KC, 2 if n == FB % 3 - 1 else 1)
                                for m in range(KC):
                                    load_expert((2 * FB + m) % RING, cols(down_w, FB, m * P), FB, 1 if m else 0)
                with turns(sp, KC // 2, {loads: 2}) as m:
                    for s in range(2):
                        load(cols(a["w_ple_gate"][l], KC, m * 2 * P + s * P), KC, P)
            for half in range(2):
                for b in range(TB):
                    sp.wait_ge(out_ready, t.out_ready.next())
                    sp.dma_start(out[0, b * P:(b + 1) * P, half * T:(half + 1) * T], x_tok[:, b, half * T:(half + 1) * T])\
                        .then_inc(out_landed, 16)
            sp.wait_ge(out_landed, 16 * 2 * TB)

        @block.gpsimd
        def _(pool):
            t = Tallies(sems)
            pool.nop().then_inc(lo_done, CREDIT)
            pool.nop().then_inc(q_staged, CREDIT)
            pool.nop().then_inc(v_staged, CREDIT)
            nc.gpsimd.memset(gate[:, 0:1], 0.0).then_inc(q_staged, t.q_staged.inc())
            nc.gpsimd.memset(gate[:, 12:13], 0.0).then_inc(v_staged, t.v_staged.inc())
            slot = [0]

            def split_lo(n, width):
                pool.wait_ge(hi_done, t.hi_done.next())
                s = slot[0]
                nc.gpsimd.tensor_tensor(w_lo[:, s, 0:n * width], w_raw[:, s, 0:n * width],
                                               w_hi[:, s, 0:n * width].bitcast(F32), ALU.subtract).then_inc(lo_done, t.lo_done.inc())
                slot[0] = 1 - s

            def attention(pairs, n_rows):
                pool.wait_ge(q_ready, t.q_ready.now())
                pool.wait_ge(k_ready, t.k_ready.now())
                pool.wait_ge(rope_ready, t.rope_ready.now())
                if n_rows == HD + 1:
                    pool.wait_ge(qrow_ready, t.qrow_ready.now())
                with turns(pool, pairs, {t.s_done: 2 * TB, t.pv_done: 2, t.q_staged: 4, t.v_staged: 4}) as j:
                    for s in range(2):
                        pool.wait_ge(q_staged, t.q_staged.now())
                        pool.wait_ge(s_done, t.s_done.now(back=TB - 1))
                        nc.gpsimd.tensor_tensor(gate[:, 0:1], gate[:, 0:1], gate[:, 0:1], ALU.add).then_inc(q_staged, t.q_staged.inc())
                        nc.gpsimd.tensor_copy(q_st[0:n_rows, s, :], q_all[0:n_rows, j * 2 + s, :]).then_inc(q_staged, t.q_staged.inc())
                        t.s_done.add(TB)
                        pool.wait_ge(v_ready, t.v_ready.now())
                        pool.wait_ge(v_staged, t.v_staged.now())
                        pool.wait_ge(pv_done, t.pv_done.now(back=1))
                        nc.gpsimd.tensor_tensor(gate[:, 12:13], gate[:, 12:13], gate[:, 12:13], ALU.add).then_inc(v_staged, t.v_staged.inc())
                        nc.gpsimd.tensor_copy(v_st[:, s], v_all[:, :, bass.ds(j * P + s * HD, HD)]).then_inc(v_staged, t.v_staged.inc())
                        t.pv_done.add()

            for l in range(DEPTH):
                with turns(pool, 3, {t.hi_done: 2, t.lo_done: 2}):
                    split_lo(KC, P), split_lo(KC, P)
                for _ in range(4):
                    split_lo(KC, P)
                pool.wait_ge(negd_ready, t.negd_ready.next())
                pool.dma_start(k_all[HD:HD + 1, :, :], scan[:, 1, :]).then_inc(negd_landed, 16)
                t.q_ready.add(3), t.k_ready.add(3), t.v_ready.add(3), t.qrow_ready.add()
                attention(3, HD + 1)
                with turns(pool, 3, {t.hi_done: 2, t.lo_done: 2}):
                    split_lo(KC, P), split_lo(KC, P)
                for _ in range(3):
                    split_lo(KC, P)
                t.rope_ready.add(6), t.v_ready.add(3), t.qrow_ready.add()
                attention(3, HD + 1)
                for _ in range(5):
                    split_lo(KC, P)
                split_lo(2, MLA_HEADS * QK_M)
                split_lo(2, MLA_HEADS * P)
                t.rope_ready.add(1 + MLA_HEADS), t.v_ready.add(4), t.k_ready.add(4)
                attention(2, QK_M)
                with turns(pool, KC, {t.hi_done: 4, t.lo_done: 4}):
                    for _ in range(4):
                        split_lo(KC, P)
                with turns(pool, KC // 2, {t.hi_done: 2, t.lo_done: 2}):
                    split_lo(KC, P), split_lo(KC, P)
                if l % 2 == 0:
                    with turns(pool, 2, {t.hi_done: EXPERT_UNITS, t.lo_done: EXPERT_UNITS}):
                        with turns(pool, FB, {t.hi_done: 2, t.lo_done: 2}):
                            split_lo(KC, P), split_lo(KC, P)
                        with turns(pool, KC // 2, {t.hi_done: 2, t.lo_done: 2}):
                            split_lo(FB, P), split_lo(FB, P)
                else:
                    split_lo(2, P)
                split_lo(2, 4 * P), split_lo(2, 4 * P)
                with turns(pool, KC // 2, {t.hi_done: 2, t.lo_done: 2}):
                    split_lo(KC, P), split_lo(KC, P)

        @block.tensor
        def _(pe):
            t = Tallies(sems)
            t.q_staged.add(), t.v_staged.add()
            pe.nop().then_inc(unit_done, CREDIT)
            pe.nop().then_inc(x_turns, CREDIT)
            pe.nop().then_inc(v_turns, CREDIT)
            pe.nop().then_inc(p_turns, CREDIT)
            pe.nop().then_inc(out_turns, CREDIT)
            pe.nop().then_inc(norm_mm, CREDIT)
            pe.nop().then_inc(rot_done, CREDIT)
            pe.nop().then_inc(s_done, CREDIT)
            pe.nop().then_inc(t_done, CREDIT)
            pe.nop().then_inc(pv_done, CREDIT)
            pe.nop().then_inc(route_done, CREDIT)
            pe.nop().then_inc(rank_done, CREDIT)
            pe.nop().then_inc(htok_turned, CREDIT)
            pe.nop().then_inc(gathered, CREDIT)
            pe.nop().then_inc(sel_turned, CREDIT)
            pe.nop().then_inc(cw_done, CREDIT)
            pe.nop().then_inc(y_turned, CREDIT)
            pe.nop().then_inc(scattered, CREDIT)
            pe.nop().then_inc(expert_unit_done, RING)
            e_landed = [t.e_landed0, t.e_landed1, t.e_landed2, t.e_landed3, t.e_landed4, t.e_landed5]
            slot = [0]

            def product(dst, s, cols, hi, lo, first=True, last=True):
                n, width = len(cols), dst.shape[0]
                for i, (c, k) in enumerate(cols):
                    wh, wl = w_hi[:, s, c:c + width], w_lo[:, s, c:c + width]
                    nc.tensor.matmul(dst, wh, hi[:, k, :], start=(first and i == 0), stop=False)
                    nc.tensor.matmul(dst, wh, lo[:, k, :], start=False, stop=False)
                    matmul = nc.tensor.matmul(dst, wl, hi[:, k, :], start=False, stop=(last and i == n - 1))
                return matmul

            def next_unit():
                pe.wait_ge(lo_done, t.lo_done.next())
                s = slot[0]
                slot[0] = 1 - s
                return s

            def block_cols(n):
                return [(k * P, k) for k in range(n)]

            def first_units(banks, width=P):
                units = [next_unit() for _ in banks]
                for k in range(KC):
                    pe.wait_ge(hlo_ready, t.hlo_ready.next())
                    for bank, unit in zip(banks, units):
                        last = product(ps[:, bank, :], unit, [(k * width, k)], h_hi, h_lo, first=(k == 0), last=(k == KC - 1))
                        if k == KC - 1:
                            last.then_inc(unit_done, t.unit_done.inc())

            def norm_total():
                pe.wait_ge(sum_ready, t.sum_ready.next(KC))
                nc.tensor.matmul(ps[:, 7, :], ones, rstd[:], start=True, stop=True).then_inc(norm_mm, t.norm_mm.inc())
                t.sq_ready.add(KC)

            def norm_sums(chunks, bank=7):
                for k in range(chunks):
                    pe.wait_ge(sq_ready, t.sq_ready.next())
                    nc.tensor.matmul(ps[:, bank, :], ones, sq[:, k % 2, :], start=(k == 0), stop=(k == chunks - 1)).then_inc(norm_mm, t.norm_mm.inc())

            def turn(dst_bank, src):
                for b in range(TB):
                    last = nc.tensor.transpose(ps[:, dst_bank, b * P:(b + 1) * P], src[:, b * P:(b + 1) * P], ident)
                return last

            def v_blocks(units):
                def turned(j):
                    pe.wait_ge(raw_ready, t.raw_ready.next())
                    if j >= 2:
                        pe.wait_ge(v_ready, t.v_ready.now(back=1))
                    turn(2 + j % 2, tmp[:, j % 2, :]).then_inc(v_turns, t.v_turns.inc())
                    t.v_ready.add()
                for j in range(units):
                    product(ps[:, j % 2, :], next_unit(), block_cols(KC), h_hi, h_lo).then_inc(unit_done, t.unit_done.inc())
                    if j:
                        turned(j - 1)
                turned(units - 1)

            def attention(pairs, n_rows):
                def scores(s, head):
                    pe.wait_ge(q_staged, t.q_staged.next(2))
                    for qb in range(TB):
                        pe.wait_ge(s_taken, t.s_taken.now(back=TB - 1))
                        nc.tensor.matmul(ps[:, qb, 0:(qb + 1) * P], q_st[0:n_rows, s, qb * P:(qb + 1) * P],
                                                k_all[0:n_rows, head, 0:(qb + 1) * P], start=True, stop=True).then_inc(s_done, t.s_done.inc())
                        t.s_taken.add()

                def turn_and_apply(s):
                    pe.wait_ge(v_staged, t.v_staged.next(2))
                    for kb in range(TB):
                        evens = kb % 2 == 0
                        if evens:
                            pe.wait_ge(pt_even, t.pt_even.now())
                        else:
                            pe.wait_ge(pt_odd, t.pt_odd.now())
                        for qb in range(kb, TB):
                            if kb == 0:
                                pe.wait_ge(p_ready, t.p_ready.next())
                            last = nc.tensor.transpose(ps[:, 4 + kb % 2, (qb - kb) * P:(qb - kb + 1) * P],
                                                       probs[:, s, qb, kb * P:(kb + 1) * P], ident)
                        last.then_inc(t_done, t.t_done.inc())
                        (t.pt_even if evens else t.pt_odd).add()
                        if kb >= 1:
                            values(s, kb - 1)
                    values(s, TB - 1)

                def values(s, kb):
                    if kb % 2 == 0:
                        pe.wait_ge(pt_even, t.pt_even.now())
                    else:
                        pe.wait_ge(pt_odd, t.pt_odd.now())
                    if kb == 0 and s == 0:
                        pe.wait_ge(olo_ready, t.olo_ready.now())
                    n = (TB - kb) * P
                    o = kb * TB * P - kb * (kb - 1) // 2 * P
                    last = nc.tensor.matmul(ps[s * HD:(s + 1) * HD, 6, kb * P:T], v_st[:, s, kb, :],
                                            pt[:, o:o + n], start=(kb == 0), stop=(kb == TB - 1), skip_group_check=True)
                    if kb == TB - 1:
                        last.then_inc(pv_done, t.pv_done.inc())

                def pair(j, last):
                    scores(1, j * 2 + 1)
                    turn_and_apply(0)
                    if not last:
                        scores(0, j * 2 + 2)
                    turn_and_apply(1)
                    t.olo_ready.add()

                pe.wait_ge(rope_ready, t.rope_ready.now())
                pe.wait_ge(q_ready, t.q_ready.now())
                pe.wait_ge(k_ready, t.k_ready.now())
                scores(0, 0)
                with turns(pe, pairs - 1, {t.q_staged: 4, t.v_staged: 4, t.s_taken: 8, t.s_done: 8, t.p_ready: 8, t.pt_even: 4,
                                           t.pt_odd: 4, t.t_done: 8, t.pv_done: 2, t.olo_ready: 1}) as j:
                    pair(j, False)
                pair(pairs - 1, True)
                pe.wait_ge(s_taken, t.s_taken.now())
                pe.wait_ge(olo_ready, t.olo_ready.now())

            pe.wait_ge(x_landed, 16)
            pe.wait_ge(table_landed, 32)
            for k in range(KC):
                if k >= 2:
                    pe.wait_ge(x_turned, t.x_turned.now(back=1))
                for b in range(TB):
                    last = nc.tensor.transpose(ps[:, k % 2, b * P:(b + 1) * P], x_tok[:, b, k * P:(k + 1) * P], ident)
                last.then_inc(x_turns, t.x_turns.inc())
                t.x_turned.add()
            pe.wait_ge(x_turned, t.x_turned.now())

            for l in range(DEPTH):
                norm_total()
                pe.wait_ge(q_ready, t.q_ready.now())
                pe.wait_ge(k_ready, t.k_ready.now())
                first_units((0, 1))
                t.q_ready.add(), t.k_ready.add()
                with turns(pe, 2, {t.lo_done: 2, t.unit_done: 2, t.q_ready: 1, t.k_ready: 1}):
                    pe.wait_ge(q_ready, t.q_ready.now())
                    product(ps[:, 0, :], next_unit(), block_cols(KC), h_hi, h_lo).then_inc(unit_done, t.unit_done.inc())
                    t.q_ready.add()
                    pe.wait_ge(k_ready, t.k_ready.now())
                    product(ps[:, 1, :], next_unit(), block_cols(KC), h_hi, h_lo).then_inc(unit_done, t.unit_done.inc())
                    t.k_ready.add()
                pe.wait_ge(q_ready, t.q_ready.now())
                pe.wait_ge(k_ready, t.k_ready.now())
                product(ps[:, 5, :], next_unit(), block_cols(KC), h_hi, h_lo).then_inc(unit_done, t.unit_done.inc())
                v_blocks(3)
                pe.wait_ge(v_ready, t.v_ready.now())
                pe.wait_ge(fz_taken, t.fz_taken.next())
                pe.wait_ge(negd_landed, 16 * (l + 1))
                pe.wait_ge(qrow_ready, t.qrow_ready.next())
                attention(3, HD + 1)
                with turns(pe, 3, {t.lo_done: 2, t.unit_done: 2, t.raw_ready: 2, t.rot_done: 2, t.rope_ready: 2}):
                    pe.wait_ge(raw_ready, t.raw_ready.now())
                    for s in range(2):
                        product(ps[:, s, :], next_unit(), block_cols(KC), h_hi, h_lo).then_inc(unit_done, t.unit_done.inc())
                    for s in range(2):
                        pe.wait_ge(raw_ready, t.raw_ready.next())
                        pe.wait_ge(rope_ready, t.rope_ready.now(back=s))
                        nc.tensor.matmul(ps[:, 2 + s, :], rot_d, tmp[:, s, :], start=True, stop=True).then_inc(rot_done, t.rot_done.inc())
                        t.rope_ready.add()
                pe.wait_ge(rope_ready, t.rope_ready.now())
                v_blocks(3)
                pe.wait_ge(v_ready, t.v_ready.now())
                pe.wait_ge(qrow_ready, t.qrow_ready.next())
                attention(3, HD + 1)
                for n in range(5):
                    product(ps[:, n, :], next_unit(), block_cols(KC), h_hi, h_lo).then_inc(unit_done, t.unit_done.inc())
                    if n == 2:
                        norm_sums(2)
                pe.wait_ge(raw_ready, t.raw_ready.next())
                nc.tensor.matmul(ps[0:QK_M, 5, :], rot_m, tmp[0:QK_M, 0, :], start=True, stop=True).then_inc(rot_done, t.rot_done.inc())
                t.rope_ready.add()
                norm_sums(2, 6)
                pe.wait_ge(hlo_ready, t.hlo_ready.next(2))
                s = next_unit()
                for hd in range(MLA_HEADS):
                    last = product(ps[0:QK_M, hd, :], s, [(k * MLA_HEADS * QK_M + hd * QK_M, k) for k in range(2)], cn_hi, cn_lo)
                last.then_inc(unit_done, t.unit_done.inc())
                for hd in range(MLA_HEADS):
                    pe.wait_ge(raw_ready, t.raw_ready.next())
                    pe.wait_ge(rope_ready, t.rope_ready.now(back=min(hd, 1)))
                    nc.tensor.matmul(ps[0:QK_M, 5 + hd % 2, :], rot_m, tmp[0:QK_M, hd % 2, :], start=True, stop=True).then_inc(rot_done, t.rot_done.inc())
                    t.rope_ready.add()
                pe.wait_ge(hlo_ready, t.hlo_ready.next(2))
                s = next_unit()
                for hd in range(MLA_HEADS):
                    last = product(ps[:, hd, :], s, [(k * MLA_HEADS * P + hd * P, k) for k in range(2)], cn_hi, cn_lo)
                last.then_inc(unit_done, t.unit_done.inc())
                pe.wait_ge(rope_ready, t.rope_ready.now())
                for hd in range(MLA_HEADS):
                    pe.wait_ge(raw_ready, t.raw_ready.next())
                    if hd >= 2:
                        pe.wait_ge(v_ready, t.v_ready.now(back=1))
                    turn(4 + hd % 2, tmp[:, hd % 2, :]).then_inc(v_turns, t.v_turns.inc())
                    t.v_ready.add()
                t.k_ready.add(4)
                pe.wait_ge(v_ready, t.v_ready.now())
                attention(2, QK_M)
                with turns(pe, KC, {t.lo_done: 4, t.unit_done: 4, t.sig_ready: 3, t.mlo_ready: 1}):
                    for b in range(3):
                        pe.wait_ge(sig_ready, t.sig_ready.now(back=2))
                        product(ps[:, b, :], next_unit(), block_cols(KC), h_hi, h_lo).then_inc(unit_done, t.unit_done.inc())
                        t.sig_ready.add()
                    s = next_unit()
                    pe.wait_ge(mlo_ready, t.mlo_ready.now())
                    for b, (c0, c1) in enumerate(((0, 3), (3, 6), (6, 8))):
                        last = product(ps[:, 3 + b, :], s, [(c * P, c) for c in range(c0, c1)], o_hi, o_lo)
                    last.then_inc(unit_done, t.unit_done.inc())
                    t.mlo_ready.add()
                with turns(pe, KC // 2, {t.lo_done: 2, t.unit_done: 2, t.x_upd: 2}):
                    for s in range(2):
                        pe.wait_ge(mlo_ready, t.mlo_ready.now(back=1))
                        pe.wait_ge(x_upd, t.x_upd.now(back=1))
                        unit = next_unit()
                        product(ps[:, 6 + s, :], unit, block_cols(KC)[:-1], m_hi, m_lo, last=False)
                        pe.wait_ge(mlo_ready, t.mlo_ready.now())
                        product(ps[:, 6 + s, :], unit, block_cols(KC)[-1:], m_hi, m_lo, first=False).then_inc(unit_done, t.unit_done.inc())
                        t.x_upd.add()
                pe.wait_ge(x_upd, t.x_upd.now())
                norm_total()
                pe.wait_ge(p_landed, 16 * (l + 1))
                for c in range(PLE // P):
                    for b in range(TB):
                        last = nc.tensor.transpose(ps[:, 4 + c, b * P:(b + 1) * P], p_tok[:, b, c * P:(c + 1) * P], ident)
                    last.then_inc(p_turns, t.p_turns.inc())
                t.plo_ready.add(2)

                def expert(half):
                    if half == 0:
                        pe.wait_ge(sig_ready, t.sig_ready.now())
                        pe.wait_ge(alo_ready, t.alo_ready.now())
                        first_units((0, 1))
                        t.sig_ready.add(), t.alo_ready.add()
                    with turns(pe, FB - 1 if half == 0 else FB, {t.lo_done: 2, t.unit_done: 2, t.sig_ready: 1, t.alo_ready: 1}):
                        pe.wait_ge(sig_ready, t.sig_ready.now())
                        product(ps[:, 0, :], next_unit(), block_cols(KC), h_hi, h_lo).then_inc(unit_done, t.unit_done.inc())
                        t.sig_ready.add()
                        pe.wait_ge(alo_ready, t.alo_ready.now())
                        product(ps[:, 1, :], next_unit(), block_cols(KC), h_hi, h_lo).then_inc(unit_done, t.unit_done.inc())
                        t.alo_ready.add()
                    with turns(pe, KC // 2, {t.lo_done: 2, t.unit_done: 2, t.x_upd: 2}):
                        for s in range(2):
                            pe.wait_ge(alo_ready, t.alo_ready.now(back=1))
                            pe.wait_ge(x_upd, t.x_upd.now(back=1))
                            unit = next_unit()
                            product(ps[:, 2 + s, :], unit, block_cols(FB)[:-1], a_hi, a_lo, last=False)
                            pe.wait_ge(alo_ready, t.alo_ready.now())
                            product(ps[:, 2 + s, :], unit, block_cols(FB)[-1:], a_hi, a_lo, first=False).then_inc(unit_done, t.unit_done.inc())
                            t.x_upd.add()

                def turn_h():
                    for bank in range(2 * TB):
                        for k in range(KC // 2):
                            last = nc.tensor.transpose(ps[:, bank, k * P:(k + 1) * P],
                                                       h_hi[:, bank % 2 * (KC // 2) + k, bank // 2 * P:(bank // 2 + 1) * P].bitcast(F32), ident)
                        last.then_inc(htok_turned, t.htok_turned.inc())
                    for bank in range(2 * TB):
                        pe.wait_ge(hthi_ready, t.hthi_ready.next())
                        for k in range(KC // 2):
                            last = nc.tensor.transpose(ps[:, bank, k * P:(k + 1) * P],
                                                       h_lo[:, bank % 2 * (KC // 2) + k, bank // 2 * P:(bank // 2 + 1) * P].bitcast(F32), ident)
                        last.then_inc(htok_turned, t.htok_turned.inc())
                    pe.wait_ge(htlo_ready, t.htlo_ready.next(2 * TB))

                def expert_product(s, chunks, acts):
                    e_landed[s].add(16)
                    pe.wait_ge(e_landed[s].sem, e_landed[s].now())
                    for k in range(chunks):
                        last = nc.tensor.matmul(ps[:, s, 0:CAP], ring[s][:, k * P:(k + 1) * P], acts[:, k, :],
                                                start=(k == 0), stop=(k == chunks - 1))
                    last.then_inc(expert_unit_done, t.expert_unit_done.inc())

                def gate_and_up(n):
                    pe.wait_ge(expert_act_ready, t.expert_act_ready.now(back=2))
                    expert_product(2 * n, KC, hg)
                    expert_product(2 * n + 1, KC, hg)
                    t.expert_act_ready.add()

                def down(m):
                    pe.wait_ge(y_taken, t.y_taken.now(back=min(m, RING - 1)))
                    pe.wait_ge(expert_act_ready, t.expert_act_ready.now())
                    expert_product((2 * FB + m) % RING, FB, ga)
                    t.y_taken.add()

                def turn_outputs(half):
                    pe.wait_ge(y_taken, t.y_taken.now(back=0 if half else 2))
                    for tile, (j0, _) in enumerate(SLOT_TILES):
                        pe.wait_ge(y32_ready, t.y32_ready.now(back=1))
                        for k in range(KC // 2):
                            last = nc.tensor.transpose(ps[:, 6 + tile, k * P:(k + 1) * P],
                                                       y_t[:, half * (KC // 2) + k, j0:j0 + P], ident)
                        last.then_inc(y_turned, t.y_turned.inc())
                        t.y32_ready.add()

                def gathered_expert():
                    pe.wait_ge(sel_ready, t.sel_ready.next())
                    for tile, (j0, _) in enumerate(SLOT_TILES):
                        for b in range(TB):
                            last = nc.tensor.transpose(ps[:, 4 + tile, b * P:(b + 1) * P],
                                                       sel[:, b, j0:j0 + P].bitcast(F32), ident)
                        last.then_inc(sel_turned, t.sel_turned.inc())
                    for pair in range(KC // 2):
                        taken = t.hgodd_ready if pair % 2 else t.hgeven_ready
                        pe.wait_ge(taken.sem, taken.now())
                        for k in (2 * pair, 2 * pair + 1):
                            for i, part in enumerate((h_hi, h_lo)):
                                for b in range(TB):
                                    last = nc.tensor.matmul(ps[:, 6 + pair % 2, k % 2 * CAP:(k % 2 + 1) * CAP],
                                                            part[:, 2 * b + k // 4, k % 4 * P:(k % 4 + 1) * P], sel[:, b, :],
                                                            start=(i == 0 and b == 0), stop=(i == 1 and b == TB - 1))
                        last.then_inc(gathered, t.gathered.inc())
                        taken.add()
                    pe.wait_ge(hgodd_ready, t.hgodd_ready.now())
                    pe.wait_ge(selt_ready, t.selt_ready.next(2))
                    pe.wait_ge(tokens_added, t.tokens_added.now())
                    pe.wait_ge(hgeven_ready, t.hgeven_ready.now())
                    for tile, (j0, _) in enumerate(SLOT_TILES):
                        for b in range(TB):
                            last = nc.tensor.matmul(ps[:, 6, tile:tile + 1], sel[:, b, j0:j0 + P].bitcast(F32),
                                                    comb_e[:, b, :], start=(b == 0), stop=(b == TB - 1))
                    last.then_inc(cw_done, t.cw_done.inc())
                    with turns(pe, FB // 3, {t.e_landed0: 16, t.e_landed1: 16, t.e_landed2: 16, t.e_landed3: 16, t.e_landed4: 16,
                                             t.e_landed5: 16, t.expert_unit_done: RING, t.expert_act_ready: 3}):
                        for n in range(3):
                            gate_and_up(n)
                    for n in range(FB % 3):
                        gate_and_up(n)
                    for m in range(KC - 2):
                        down(m)
                    turn_outputs(0)
                    for m in range(KC - 2, KC):
                        down(m)
                    turn_outputs(1)
                    for m in range(KC):
                        if m % 4 == 0:
                            pe.wait_ge(ylo_ready, t.ylo_ready.next(2))
                        pe.wait_ge(tokens_added, t.tokens_added.now(back=min(m, 3)))
                        for tile, (_, r0) in enumerate(SLOT_TILES):
                            for part in (y_hi, y_lo):
                                last = nc.tensor.matmul(ps[:, m % 4, :], part[r0:P, tile, m * P:(m + 1) * P],
                                                        sel_t[r0:P, tile, :], start=(tile == 0 and part is y_hi),
                                                        stop=(tile == 1 and part is y_lo))
                        last.then_inc(scattered, t.scattered.inc())
                        t.tokens_added.add()

                if l % 2 == 0:
                    for half in range(2):
                        expert(half)
                else:
                    first_units((6,), EXPERTS)
                    pe.wait_ge(plo_ready, t.plo_ready.now())
                    pe.wait_ge(logits_taken, t.logits_taken.next())
                    for b in range(TB):
                        last = nc.tensor.matmul(ps[:, 5, b * EXPERTS:(b + 1) * EXPERTS], tmp[0:EXPERTS, 0, b * P:(b + 1) * P],
                                                ident[0:EXPERTS, 0:EXPERTS], start=True, stop=True)
                    last.then_inc(route_done, t.route_done.inc())
                    pe.wait_ge(logits_taken, t.logits_taken.next())
                    turn_h()
                    pe.wait_ge(mask_ready, t.mask_ready.next())
                    for b in range(TB):
                        for before_b in range(b + 1):
                            lhs = const[:, K_BEFORE:K_BEFORE + P] if before_b == b else ones
                            nc.tensor.matmul(ps[:, 5, b * EXPERTS:(b + 1) * EXPERTS], lhs, route[:, 3, before_b, :],
                                             start=(before_b == 0), stop=(before_b == b))
                    for b in range(TB):
                        last = nc.tensor.matmul(ps[:, 5, TB * EXPERTS:(TB + 1) * EXPERTS], ones, route[:, 3, b, :],
                                                start=(b == 0), stop=(b == TB - 1))
                    last.then_inc(rank_done, t.rank_done.inc())
                    pe.wait_ge(tops_ready, t.tops_ready.next())
                    per_expert = {t.e_landed0: 80, t.e_landed1: 80, t.e_landed2: 80, t.e_landed3: 80, t.e_landed4: 80,
                                  t.e_landed5: 80, t.expert_unit_done: EXPERT_UNITS, t.expert_act_ready: FB, t.tokens_added: KC,
                                  t.sel_turned: 2, t.hgeven_ready: 2, t.hgodd_ready: 2, t.gathered: KC // 2, t.cw_done: 1,
                                  t.sel_ready: 1, t.selt_ready: 2, t.y_taken: KC, t.y_turned: 4, t.y32_ready: 4,
                                  t.ylo_ready: 4, t.scattered: KC}
                    with turns(pe, ROUNDS, {c: EXPERTS * n for c, n in per_expert.items()} | {t.sel_ready: EXPERTS + 1}) as r:
                        with pe.If(pe.value_load(tops[0:1, bass.ds(r, 1)]) > 0):
                            with turns(pe, EXPERTS, per_expert):
                                gathered_expert()
                            t.sel_ready.add()
                    pe.wait_ge(moe_done, t.moe_done.next())
                pe.wait_ge(x_upd, t.x_upd.now())
                if l % 2 == 0:
                    norm_total()
                pe.wait_ge(plo_ready, t.plo_ready.now())
                for half in range(2):
                    s = next_unit()
                    if l % 2 and half:
                        norm_total()
                    for n in range(4):
                        if half * 4 + n == 7:
                            pe.wait_ge(pp_ready, t.pp_ready.now() + 1)
                        last = product(ps[:, (half * 4 + n) % 7, :], s, [(c * 4 * P + n * P, c) for c in range(2)], p_hi, p_lo)
                    last.then_inc(unit_done, t.unit_done.inc())
                pe.wait_ge(pp_ready, t.pp_ready.now() + 4)
                t.pp_ready.add(KC)
                first_units((2, 3))
                t.x_upd.add(2)
                with turns(pe, KC // 2 - 1, {t.lo_done: 2, t.unit_done: 2, t.x_upd: 2}):
                    for s in range(2):
                        pe.wait_ge(x_upd, t.x_upd.now(back=1))
                        product(ps[:, 2 + s, :], next_unit(), block_cols(KC), h_hi, h_lo).then_inc(unit_done, t.unit_done.inc())
                        t.x_upd.add()
                pe.wait_ge(x_upd, t.x_upd.now())
                t.sig_ready.add(KC)
            norm_total()
            for half in range(2):
                pe.wait_ge(xn_ready, t.xn_ready.next(KC // 2))
                for b in range(TB):
                    pe.wait_ge(out_ready, t.out_ready.now(back=3))
                    for k in range(KC // 2):
                        last = nc.tensor.transpose(ps[:, b, k * P:(k + 1) * P], x[:, half * KC // 2 + k, b * P:(b + 1) * P], ident)
                    last.then_inc(out_turns, t.out_turns.inc())
                    t.out_ready.add()

        @block.scalar
        def _(act):
            t = Tallies(sems)
            act.nop().then_inc(hi_done, CREDIT)
            act.nop().then_inc(act_step, CREDIT)
            act.nop().then_inc(sq_ready, CREDIT)
            act.nop().then_inc(root_ready, CREDIT)
            act.nop().then_inc(hn_ready, CREDIT)
            act.nop().then_inc(raw_ready, CREDIT)
            act.nop().then_inc(k_ready, CREDIT)
            act.nop().then_inc(sig_ready, CREDIT)
            act.nop().then_inc(mhi_ready, CREDIT)
            act.nop().then_inc(ahi_ready, CREDIT)
            act.nop().then_inc(exp_done, CREDIT)
            act.nop().then_inc(pt_even, CREDIT)
            act.nop().then_inc(ohi_ready, CREDIT)
            act.nop().then_inc(fz_ready, CREDIT)
            act.nop().then_inc(phi_ready, CREDIT)
            act.nop().then_inc(pp_ready, CREDIT)
            act.nop().then_inc(share_ready, CREDIT)
            act.nop().then_inc(hthi_ready, CREDIT)
            act.nop().then_inc(hgeven_ready, CREDIT)
            act.nop().then_inc(yhi_ready, CREDIT)
            act.nop().then_inc(out_ready, CREDIT)
            act.nop().then_inc(silu_ready, CREDIT)
            act.nop().then_inc(selt_ready, CREDIT)
            landed = [t.w_landed0, t.w_landed1]
            slot = [0]
            A = nc.scalar.activation

            def split_hi(dmas=1):
                s = slot[0]
                landed[s].add(16 * dmas)
                act.wait_ge(landed[s].sem, landed[s].now())
                act.wait_ge(unit_done, t.hi_done.now(back=1))
                A(w_hi[:, s, :], w_raw[:, s, :], ACT.Copy).then_inc(hi_done, t.hi_done.inc())
                slot[0] = 1 - s

            def square(k, s):
                act.wait_ge(sum_ready, t.sum_ready.now(back=1))
                A(sq[:, s, :], x[:, k, :], ACT.Square).then_inc(sq_ready, t.sq_ready.inc())
                t.sum_ready.add()

            def squares(src, chunks):
                for k in range(chunks):
                    act.wait_ge(norm_mm, t.norm_mm.now(back=1))
                    A(sq[:, k % 2, :], src[:, k, :], ACT.Square).then_inc(sq_ready, t.sq_ready.inc())
                    t.norm_mm.add()

            def root(bank, dim):
                act.wait_ge(norm_mm, t.norm_mm.now())
                A(rstd[:], ps[:, bank, :], ACT.Sqrt, bias=const[:, K_EPS:K_EPS + 1], scale=1.0 / dim).then_inc(root_ready, t.root_ready.inc())

            def angle_tables(n, cos_t, sin_t):
                act.wait_ge(ang_ready, t.ang_ready.next())
                A(sin_t[:], trig[:, n, :], ACT.Sin)
                A(trig[:, 2, :], trig[:, n, :], ACT.Abs).then_inc(act_step, t.act_step.inc())
                act.wait_ge(act_step, t.act_step.now())
                A(cos_t[:], trig[:, 2, :], ACT.Sin, scale=-1.0, bias=const[:, K_HALFPI:K_HALFPI + 1]).then_inc(act_step, t.act_step.inc())
                act.wait_ge(act_step, t.act_step.now())

            def norm_hi(blocks, hi):
                for k in blocks:
                    act.wait_ge(hf_ready, t.hf_ready.next())
                    A(hi[:, k, :], tmp[:, 2 + k % 2, :], ACT.Copy).then_inc(hn_ready, t.hn_ready.inc())

            def v_blocks(units):
                for j in range(units):
                    split_hi()
                    act.wait_ge(unit_done, t.unit_done.next())
                    act.wait_ge(v_turns, t.v_turns.now(back=min(j, 1)))
                    A(tmp[:, j % 2, :], ps[:, j % 2, :], ACT.Copy).then_inc(raw_ready, t.raw_ready.inc())
                    t.v_turns.add()

            def attention(pairs, pair0):
                def exponentials(s, blocks=range(TB)):
                    if blocks[0] == 0:
                        act.wait_ge(neg_ready, t.neg_ready.next())
                    for qb in blocks:
                        n = (qb + 1) * P
                        A(probs[:, s, qb, 0:n], probs[:, s, qb, 0:n], ACT.Exp, bias=sneg[:, s, qb:qb + 1],
                                 accum_out=ssum[:, s, qb:qb + 1]).then_inc(exp_done, t.exp_done.inc())

                def even_block(kb):
                    act.wait_ge(t_done, t.t_done.next())
                    act.wait_ge(pv_done, t.pv_done.now())
                    n, o = (TB - kb) * P, kb * TB * P - kb * (kb - 1) // 2 * P
                    A(pt[:, o:o + n], ps[:, 4, 0:n], ACT.Copy).then_inc(pt_even, t.pt_even.inc())
                    t.t_done.add()
                    if kb == TB - 2:
                        t.pv_done.add()

                def pair(j, last):
                    even_block(0)
                    exponentials(1, (0, 1))
                    even_block(2)
                    exponentials(1, (2, 3))
                    even_block(0)
                    if not last:
                        exponentials(0, (0, 1))
                    even_block(2)
                    if not last:
                        exponentials(0, (2, 3))
                    act.wait_ge(pv_done, t.pv_done.now())
                    A(o_hi[:, pair0 + j, :], ps[:, 6, :], ACT.Copy).then_inc(ohi_ready, t.ohi_ready.inc())

                exponentials(0)
                with turns(act, pairs - 1, {t.neg_ready: 2, t.exp_done: 8, t.t_done: 8, t.pv_done: 2, t.pt_even: 4,
                                            t.ohi_ready: 1}) as j:
                    pair(j, False)
                pair(pairs - 1, True)

            act.wait_ge(table_landed, 32)
            for k in range(KC):
                act.wait_ge(x_turned, t.x_turned.next())
                square(k, k % 2)
            for _ in range(2):
                split_hi()

            for l in range(DEPTH):
                last_layer = l == DEPTH - 1
                t.norm_mm.add()
                root(7, D)
                norm_hi(range(KC), h_hi)
                if l == 0:
                    angle_tables(0, cos_d, sin_d)
                with turns(act, 3, {t.hi_done: 2, t.w_landed0: 16, t.w_landed1: 16, t.unit_done: 2, t.k_ready: 1}) as j:
                    split_hi()
                    t.unit_done.add()
                    split_hi()
                    act.wait_ge(unit_done, t.unit_done.next())
                    A(k_all[0:HD, j * 2, :], ps[0:HD, 1, :], ACT.Copy)
                    A(k_all[0:HD, j * 2 + 1, :], ps[HD:P, 1, :], ACT.Copy).then_inc(k_ready, t.k_ready.inc())
                split_hi()
                t.unit_done.add()
                if l == 0:
                    angle_tables(1, cos_m, sin_m)
                act.wait_ge(fz_taken, t.fz_taken.next())
                A(scan_t[:, 1, :], scan_t[:, 0, :], ACT.Abs).then_inc(act_step, t.act_step.inc())
                act.wait_ge(act_step, t.act_step.now())
                A(scan_t[:, 2, :], scan_t[:, 1, :], ACT.Exp, scale=-1.0).then_inc(act_step, t.act_step.inc())
                act.wait_ge(act_step, t.act_step.now())
                A(scan_t[:, 3, :], scan_t[:, 2, :], ACT.Ln, bias=1.0).then_inc(fz_ready, t.fz_ready.inc())
                v_blocks(3)
                attention(3, 0)
                with turns(act, 3, {t.hi_done: 2, t.w_landed0: 16, t.w_landed1: 16, t.unit_done: 2, t.raw_ready: 2, t.rope_ready: 2}):
                    for s in range(2):
                        split_hi()
                        act.wait_ge(unit_done, t.unit_done.next())
                        act.wait_ge(rope_ready, t.rope_ready.now(back=s))
                        A(tmp[:, s, :], ps[:, s, :], ACT.Copy, scale=HD**-0.5 if s == 0 else 1.0).then_inc(raw_ready, t.raw_ready.inc())
                    t.rope_ready.add(2)
                act.wait_ge(rope_ready, t.rope_ready.now())
                v_blocks(3)
                attention(3, 3)
                for n in range(5):
                    split_hi()
                    act.wait_ge(unit_done, t.unit_done.next())
                    if n == 4:
                        act.wait_ge(v_turns, t.v_turns.now())
                        A(tmp[0:QK_M, 0, :], ps[0:QK_M, 4, :], ACT.Copy).then_inc(raw_ready, t.raw_ready.inc())
                    else:
                        dst = cq_raw if n < 2 else ckv_raw
                        A(dst[:, n % 2, :], ps[:, n, :], ACT.Copy).then_inc(act_step, t.act_step.inc())
                    if n in (1, 3):
                        act.wait_ge(act_step, t.act_step.now())
                        squares(dst, 2)
                    if n == 2:
                        root(7, RANK)
                        norm_hi(range(2), cn_hi)
                root(6, RANK)
                split_hi()
                act.wait_ge(unit_done, t.unit_done.next())
                t.rope_ready.add()
                for hd in range(MLA_HEADS):
                    act.wait_ge(rope_ready, t.rope_ready.now(back=min(hd, 1)))
                    A(tmp[0:QK_M, hd % 2, :], ps[0:QK_M, hd, :], ACT.Copy, scale=QK_M**-0.5).then_inc(raw_ready, t.raw_ready.inc())
                    t.rope_ready.add()
                norm_hi(range(2), cn_hi)
                split_hi()
                act.wait_ge(unit_done, t.unit_done.next())
                act.wait_ge(rope_ready, t.rope_ready.now())
                for hd in range(MLA_HEADS):
                    A(k_all[0:NOPE, hd, :], ps[0:NOPE, hd, :], ACT.Copy).then_inc(k_ready, t.k_ready.inc())
                    act.wait_ge(v_turns, t.v_turns.now(back=min(hd, 1)))
                    A(tmp[:, hd % 2, :], ps[:, hd, :], ACT.Copy).then_inc(raw_ready, t.raw_ready.inc())
                    t.v_turns.add()
                attention(2, 6)
                with turns(act, KC, {t.hi_done: 4, t.w_landed0: 32, t.w_landed1: 64, t.unit_done: 4, t.sig_ready: 3,
                                     t.m_ready: 1, t.mhi_ready: 1, t.mlo_ready: 1}) as m:
                    for b in range(3):
                        split_hi(3 if b == 1 else 1)
                        act.wait_ge(unit_done, t.unit_done.next())
                        act.wait_ge(mlo_ready, t.mlo_ready.now())
                        A(sg[:, b, :], ps[:, b, :], ACT.Sigmoid).then_inc(sig_ready, t.sig_ready.inc())
                    split_hi()
                    t.unit_done.add()
                    act.wait_ge(m_ready, t.m_ready.next())
                    A(m_hi[:, m, :], tmp[:, 0, :], ACT.Copy).then_inc(mhi_ready, t.mhi_ready.inc())
                    t.mlo_ready.add()
                with turns(act, KC // 2, {t.hi_done: 2, t.w_landed0: 16, t.w_landed1: 16, t.unit_done: 2, t.x_upd: 2,
                                          t.sum_ready: 2, t.sq_ready: 2}) as m:
                    for s in range(2):
                        split_hi()
                        t.unit_done.add()
                        act.wait_ge(x_upd, t.x_upd.next())
                        square(m * 2 + s, s)
                t.norm_mm.add()
                root(7, D)
                for c in range(PLE // P):
                    act.wait_ge(p_turns, t.p_turns.next())
                    A(p_hi[:, c, :], ps[:, 4 + c, :], ACT.Copy).then_inc(phi_ready, t.phi_ready.inc())
                norm_hi(range(KC), h_hi)

                def expert(half):
                    with turns(act, FB, {t.hi_done: 2, t.w_landed0: 16, t.w_landed1: 16, t.unit_done: 2, t.af_ready: 1,
                                         t.sig_ready: 1, t.ahi_ready: 1}) as f:
                        split_hi()
                        act.wait_ge(unit_done, t.unit_done.next())
                        act.wait_ge(af_ready, t.af_ready.now())
                        A(sg[:, 0, :], ps[:, 0, :], ACT.Silu).then_inc(sig_ready, t.sig_ready.inc())
                        split_hi()
                        t.unit_done.add()
                        act.wait_ge(af_ready, t.af_ready.next())
                        A(a_hi[:, f, :], tmp[:, 0, :], ACT.Copy).then_inc(ahi_ready, t.ahi_ready.inc())
                    if half == 0:
                        with turns(act, KC // 2, {t.hi_done: 2, t.w_landed0: 16, t.w_landed1: 16, t.unit_done: 2}):
                            for s in range(2):
                                split_hi()
                                t.unit_done.add()
                        t.x_upd.add(KC)
                    else:
                        with turns(act, KC // 2, {t.hi_done: 2, t.w_landed0: 16, t.w_landed1: 16, t.unit_done: 2, t.x_upd: 2,
                                                  t.sum_ready: 2, t.sq_ready: 2}) as m:
                            for s in range(2):
                                split_hi()
                                t.unit_done.add()
                                act.wait_ge(x_upd, t.x_upd.next())
                                square(m * 2 + s, s)

                def gate_block(n):
                    act.wait_ge(expert_unit_done, t.expert_unit_done.next())
                    A(silu[:, n, :], ps[:, 2 * n, 0:CAP], ACT.Silu).then_inc(silu_ready, t.silu_ready.inc())
                    t.expert_unit_done.add()

                def upper_outputs(half):
                    for tile in range(2):
                        act.wait_ge(y32_ready, t.y32_ready.next())
                        A(y_hi[:, tile, half * T:(half + 1) * T], tmp[:, 2 * half + tile, :], ACT.Copy)\
                            .then_inc(yhi_ready, t.yhi_ready.inc())

                def gathered_expert():
                    for tile in range(2):
                        act.wait_ge(sel_turned, t.sel_turned.next())
                        A(sel_t[:, tile, :], ps[:, 4 + tile, :], ACT.Copy).then_inc(selt_ready, t.selt_ready.inc())
                    for pair in range(0, KC // 2, 2):
                        act.wait_ge(gathered, t.gathered.next())
                        A(hg[:, 2 * pair:2 * pair + 2, :], ps[:, 6, 0:2 * CAP].rearrange("p (k n) -> p k n", k=2), ACT.Copy)\
                            .then_inc(hgeven_ready, t.hgeven_ready.inc())
                        t.gathered.add()
                    with turns(act, FB // 3, {t.expert_unit_done: RING, t.silu_ready: 3}):
                        for n in range(3):
                            gate_block(n)
                    for n in range(FB % 3):
                        gate_block(n)
                    t.expert_unit_done.add(KC)
                    upper_outputs(0)
                    upper_outputs(1)

                if l % 2 == 0:
                    for half in range(2):
                        expert(half)
                else:
                    split_hi()
                    t.unit_done.add()
                    act.wait_ge(htok_turned, t.htok_turned.next(2 * TB))
                    for bank in range(2 * TB):
                        A(h_hi[:, bank, :], ps[:, bank, :], ACT.Copy).then_inc(hthi_ready, t.hthi_ready.inc())
                    act.wait_ge(gap_ready, t.gap_ready.next())
                    A(route[:, 9, :, 0:1], route[:, 8, :, 0:1], ACT.Exp).then_inc(share_ready, t.share_ready.inc())
                    act.wait_ge(tops_ready, t.tops_ready.next())
                    per_expert = {t.sel_turned: 2, t.selt_ready: 2, t.gathered: KC // 2, t.hgeven_ready: 2, t.silu_ready: FB,
                                  t.expert_unit_done: EXPERT_UNITS, t.y32_ready: 4, t.yhi_ready: 4}
                    with turns(act, ROUNDS, {c: EXPERTS * n for c, n in per_expert.items()}) as r:
                        with act.If(act.value_load(tops[0:1, bass.ds(r, 1)]) > 0):
                            with turns(act, EXPERTS, per_expert):
                                gathered_expert()
                    act.wait_ge(moe_done, t.moe_done.next())
                    for k in range(KC):
                        square(k, k % 2)
                t.norm_mm.add()
                root(7, D)

                def embedded(n):
                    A(pp[:, n, :], ps[:, n % 7, :], ACT.Copy).then_inc(pp_ready, t.pp_ready.inc())
                split_hi()
                act.wait_ge(unit_done, t.unit_done.next())
                for k in range(2):
                    norm_hi((k,), h_hi)
                    embedded(k)
                norm_hi((2,), h_hi)
                split_hi()
                act.wait_ge(unit_done, t.unit_done.next())
                for k in range(3, KC):
                    embedded(k - 1)
                    norm_hi((k,), h_hi)
                embedded(KC - 1)

                def gates(split, block):
                    for s in range(2):
                        if split:
                            split_hi()
                        act.wait_ge(unit_done, t.unit_done.next())
                        act.wait_ge(x_upd, t.x_upd.now(back=1))
                        A(sg[:, s, :], ps[:, 2 + s, :], ACT.Sigmoid).then_inc(sig_ready, t.sig_ready.inc())
                        act.wait_ge(x_upd, t.x_upd.next())
                        square(block + s, s)

                gate_turns = KC // 2 - last_layer
                with turns(act, gate_turns, {t.hi_done: 2, t.w_landed0: 16, t.w_landed1: 16, t.unit_done: 2, t.x_upd: 2, t.sig_ready: 2,
                                            t.sum_ready: 2, t.sq_ready: 2}) as m:
                    gates(True, m * 2)
                if last_layer:
                    gates(False, KC - 2)
                act.wait_ge(x_upd, t.x_upd.now())
            t.norm_mm.add()
            root(7, D)
            for half in range(2):
                for b in range(TB):
                    act.wait_ge(out_turns, t.out_turns.next())
                    A(x_tok[:, b, half * T:(half + 1) * T], ps[:, b, :], ACT.Copy).then_inc(out_ready, t.out_ready.inc())

        @block.vector
        def _(dve):
            t = Tallies(sems)
            dve.nop().then_inc(dve_step, CREDIT)
            dve.nop().then_inc(raw_zeroed, CREDIT)
            dve.nop().then_inc(x_turned, CREDIT)
            dve.nop().then_inc(ang_ready, CREDIT)
            dve.nop().then_inc(hf_ready, CREDIT)
            dve.nop().then_inc(sum_ready, CREDIT)
            dve.nop().then_inc(hlo_ready, CREDIT)
            dve.nop().then_inc(q_ready, CREDIT)
            dve.nop().then_inc(rope_ready, CREDIT)
            dve.nop().then_inc(v_ready, CREDIT)
            dve.nop().then_inc(fz_taken, CREDIT)
            dve.nop().then_inc(negd_ready, CREDIT)
            dve.nop().then_inc(s_taken, CREDIT)
            dve.nop().then_inc(neg_ready, CREDIT)
            dve.nop().then_inc(p_ready, CREDIT)
            dve.nop().then_inc(pt_odd, CREDIT)
            dve.nop().then_inc(olo_ready, CREDIT)
            dve.nop().then_inc(m_ready, CREDIT)
            dve.nop().then_inc(mlo_ready, CREDIT)
            dve.nop().then_inc(x_upd, CREDIT)
            dve.nop().then_inc(af_ready, CREDIT)
            dve.nop().then_inc(alo_ready, CREDIT)
            dve.nop().then_inc(plo_ready, CREDIT)
            dve.nop().then_inc(xn_ready, CREDIT)
            dve.nop().then_inc(comb_ready, CREDIT)
            dve.nop().then_inc(logits_taken, CREDIT)
            dve.nop().then_inc(qrow_ready, CREDIT)
            dve.nop().then_inc(gap_ready, CREDIT)
            dve.nop().then_inc(mask_ready, CREDIT)
            dve.nop().then_inc(tops_ready, CREDIT)
            dve.nop().then_inc(htlo_ready, CREDIT)
            dve.nop().then_inc(sel_ready, CREDIT)
            dve.nop().then_inc(hgodd_ready, CREDIT)
            dve.nop().then_inc(expert_act_ready, CREDIT)
            dve.nop().then_inc(tokens_added, CREDIT)
            dve.nop().then_inc(moe_done, CREDIT)
            dve.nop().then_inc(cw_ready, CREDIT)
            dve.nop().then_inc(y_taken, CREDIT)
            dve.nop().then_inc(y32_ready, CREDIT)
            dve.nop().then_inc(ylo_ready, CREDIT)
            dve.nop().then_inc(moe_step, CREDIT)
            V = nc.vector

            def clear_sum():
                V.memset(rstd[:], 0.0).then_inc(dve_step, t.dve_step.inc())
                dve.wait_ge(dve_step, t.dve_step.now())

            def add_square(s):
                dve.wait_ge(sq_ready, t.sq_ready.next())
                dve.wait_ge(sum_ready, t.sum_ready.now())
                V.tensor_tensor(rstd[:], rstd[:], sq[:, s, :], ALU.add).then_inc(sum_ready, t.sum_ready.inc())

            def inverse_root():
                dve.wait_ge(root_ready, t.root_ready.next())
                V.reciprocal(rstd[:], rstd[:]).then_inc(dve_step, t.dve_step.inc())
                dve.wait_ge(dve_step, t.dve_step.now())

            def norm(src, chunks, gain, hi, lo, inverted=False):
                if not inverted:
                    inverse_root()

                def lower(k):
                    dve.wait_ge(hn_ready, t.hn_ready.next())
                    V.tensor_tensor(lo[:, k, :], tmp[:, 2 + k % 2, :], hi[:, k, :].bitcast(F32), ALU.subtract).then_inc(hlo_ready, t.hlo_ready.inc())
                for k in range(chunks):
                    dve.wait_ge(hlo_ready, t.hlo_ready.now())
                    V.scalar_tensor_tensor(out=tmp[:, 2 + k % 2, :], in0=src[:, k, :], scalar=gain[:, k:k + 1],
                                                  in1=rstd[:], op0=ALU.mult, op1=ALU.mult).then_inc(hf_ready, t.hf_ready.inc())
                    if k:
                        dve.wait_ge(hf_ready, t.hf_ready.now(back=1))
                        lower(k - 1)
                dve.wait_ge(hf_ready, t.hf_ready.now())
                lower(chunks - 1)

            def rope(s, bank, n_rows, cos_t, sin_t, outs):
                dve.wait_ge(raw_ready, t.raw_ready.next())
                dve.wait_ge(rope_ready, t.rope_ready.now())
                V.tensor_tensor(tmp[0:n_rows, 2, :], tmp[0:n_rows, s, :], cos_t[0:n_rows, :], ALU.mult)
                dve.wait_ge(rot_done, t.rot_done.next())
                V.tensor_tensor(tmp[0:n_rows, 3, :], ps[0:n_rows, bank, :], sin_t[0:n_rows, :], ALU.mult).then_inc(dve_step, t.dve_step.inc())
                dve.wait_ge(dve_step, t.dve_step.now())
                for dst, r0, r1 in outs:
                    last = V.tensor_tensor(dst, tmp[r0:r1, 2, :], tmp[r0:r1, 3, :], ALU.add)
                last.then_inc(rope_ready, t.rope_ready.inc())

            def v_blocks(units):
                for j in range(units):
                    t.unit_done.add(), t.raw_ready.add()
                    dve.wait_ge(v_turns, t.v_turns.next())
                    V.tensor_copy(v_all[:, :, j * P:(j + 1) * P],
                                         ps[:, 2 + j % 2, :].rearrange("p (b n) -> p b n", b=TB)).then_inc(v_ready, t.v_ready.inc())

            def attention(pairs, pair0, kind):
                def maxima(s):
                    for qb in range(TB):
                        n = (qb + 1) * P
                        dve.wait_ge(s_done, t.s_done.next())
                        V.memset(gate[:, 4 + s * TB + qb:5 + s * TB + qb], 0.0)
                        V.tensor_tensor_reduce(out=probs[:, s, qb, 0:n], in0=ps[:, qb, 0:n],
                                                      in1=const[:, K_BIAS + kind * T + T - n:K_BIAS + (kind + 1) * T],
                                                      scale=1.0, scalar=-3e38, op0=ALU.add, op1=ALU.max,
                                                      accum_out=smax[:, s, qb:qb + 1]).then_inc(s_taken, t.s_taken.inc())
                    dve.wait_ge(s_taken, t.s_taken.now())
                    V.tensor_scalar(sneg[:, s, :], smax[:, s, :], -1.0, None, ALU.mult).then_inc(neg_ready, t.neg_ready.inc())

                def normalise(s):
                    dve.wait_ge(exp_done, t.exp_done.next(TB))
                    V.reciprocal(srec[:, s, :], ssum[:, s, :]).then_inc(dve_step, t.dve_step.inc())
                    dve.wait_ge(dve_step, t.dve_step.now())
                    for qb in range(TB):
                        n = (qb + 1) * P
                        V.tensor_scalar(probs[:, s, qb, 0:n], probs[:, s, qb, 0:n], srec[:, s, qb:qb + 1], None, ALU.mult).then_inc(p_ready, t.p_ready.inc())

                def odd_blocks(s):
                    for kb in range(1, TB, 2):
                        t.t_done.add()
                        dve.wait_ge(t_done, t.t_done.next())
                        dve.wait_ge(pv_done, t.pv_done.now())
                        n, o = (TB - kb) * P, kb * TB * P - kb * (kb - 1) // 2 * P
                        V.tensor_copy(pt[:, o:o + n], ps[:, 5, 0:n]).then_inc(pt_odd, t.pt_odd.inc())
                    t.pv_done.add()

                def pair(j, last):
                    normalise(0)
                    maxima(1)
                    odd_blocks(0)
                    normalise(1)
                    if not last:
                        maxima(0)
                    odd_blocks(1)
                    dve.wait_ge(ohi_ready, t.ohi_ready.next())
                    V.tensor_tensor(o_lo[:, pair0 + j, :], ps[:, 6, :], o_hi[:, pair0 + j, :].bitcast(F32), ALU.subtract).then_inc(olo_ready, t.olo_ready.inc())

                maxima(0)
                with turns(dve, pairs - 1, {t.s_done: 8, t.s_taken: 8, t.neg_ready: 2, t.exp_done: 8, t.dve_step: 2, t.p_ready: 8,
                                            t.t_done: 8, t.pv_done: 2, t.pt_odd: 4, t.ohi_ready: 1, t.olo_ready: 1}) as j:
                    pair(j, False)
                pair(pairs - 1, True)

            def routing():
                r = lambda n, b: route[:, n, b, :]
                V.tensor_copy(tmp[0:EXPERTS, 0, :], ps[0:EXPERTS, 6, :]).then_inc(logits_taken, t.logits_taken.inc())
                dve.wait_ge(route_done, t.route_done.next())
                V.tensor_copy(route[:, 0], ps[:, 5, 0:TB * EXPERTS].rearrange("p (b e) -> p b e", b=TB)).then_inc(logits_taken, t.logits_taken.inc())
                dve.wait_ge(logits_taken, t.logits_taken.now())
                iota = const[:, K_IOTA:K_IOTA + EXPERTS]
                for n, src, index, hot in ((1, 0, 3, 4), (2, 5, 6, 7)):
                    for b in range(TB):
                        last = V.max(out=r(n, b), in_=r(src, b))
                    last.then_inc(dve_step, t.dve_step.inc())
                    dve.wait_ge(dve_step, t.dve_step.now())
                    for b in range(TB):
                        last = V.max_index(out=route_i[:, b, :], in_max=r(n, b), in_values=r(src, b))
                    last.then_inc(dve_step, t.dve_step.inc())
                    dve.wait_ge(dve_step, t.dve_step.now())
                    V.tensor_copy(route[:, index], route_i[:]).then_inc(dve_step, t.dve_step.inc())
                    dve.wait_ge(dve_step, t.dve_step.now())
                    for b in range(TB):
                        last = V.tensor_scalar(r(hot, b), iota, r(index, b)[:, 0:1], None, ALU.is_equal)
                    last.then_inc(dve_step, t.dve_step.inc())
                    dve.wait_ge(dve_step, t.dve_step.now())
                    if n == 1:
                        V.scalar_tensor_tensor(out=route[:, 5], in0=route[:, 4], scalar=MASKED, in1=route[:, 0], op0=ALU.mult, op1=ALU.add).then_inc(dve_step, t.dve_step.inc())
                        dve.wait_ge(dve_step, t.dve_step.now())
                V.tensor_tensor(route[:, 8, :, 0:1], route[:, 2, :, 0:1], route[:, 1, :, 0:1], ALU.subtract).then_inc(gap_ready, t.gap_ready.inc())
                dve.wait_ge(share_ready, t.share_ready.next())
                V.tensor_scalar(route[:, 8, :, 1:2], route[:, 9, :, 0:1], 1.0, None, ALU.add).then_inc(dve_step, t.dve_step.inc())
                dve.wait_ge(dve_step, t.dve_step.now())
                V.reciprocal(route[:, 10, :, 0:1], route[:, 8, :, 1:2]).then_inc(dve_step, t.dve_step.inc())
                dve.wait_ge(dve_step, t.dve_step.now())
                V.tensor_tensor(route[:, 10, :, 1:2], route[:, 10, :, 0:1], route[:, 9, :, 0:1], ALU.mult).then_inc(dve_step, t.dve_step.inc())
                dve.wait_ge(dve_step, t.dve_step.now())
                for b in range(TB):
                    last = V.tensor_scalar(r(11, b), r(7, b), r(10, b)[:, 1:2], None, ALU.mult)
                last.then_inc(dve_step, t.dve_step.inc())
                dve.wait_ge(dve_step, t.dve_step.now())
                for b in range(TB):
                    last = V.scalar_tensor_tensor(out=r(11, b), in0=r(4, b), scalar=r(10, b)[:, 0:1], in1=r(11, b), op0=ALU.mult, op1=ALU.add)
                last.then_inc(comb_ready, t.comb_ready.inc())
                V.tensor_tensor(route[:, 3], route[:, 4], route[:, 7], ALU.add).then_inc(mask_ready, t.mask_ready.inc())
                dve.wait_ge(comb_ready, t.comb_ready.now())
                V.tensor_copy(comb_tab[:, :, 0:EXPERTS], route[:, 11])
                dve.wait_ge(htok_turned, t.htok_turned.next(4 * TB))
                for bank in range(2 * TB):
                    V.tensor_copy(h_lo[:, bank, :], ps[:, bank, :]).then_inc(htlo_ready, t.htlo_ready.inc())
                dve.wait_ge(rank_done, t.rank_done.next())
                dve.wait_ge(mask_ready, t.mask_ready.now())
                V.scalar_tensor_tensor(out=route[:, 6], in0=ps[:, 5, 0:TB * EXPERTS].rearrange("p (b e) -> p b e", b=TB), scalar=1.0,
                                       in1=route[:, 3], op0=ALU.add, op1=ALU.mult).then_inc(dve_step, t.dve_step.inc())
                dve.wait_ge(dve_step, t.dve_step.now())
                V.tensor_scalar(rank_tab[:, :, 0:EXPERTS], route[:, 6], 1.0, None, ALU.subtract)
                V.reduce_max(gate[0:1, 3:4], ps[0:1, 5, TB * EXPERTS:(TB + 1) * EXPERTS], mybir.AxisListType.X)\
                    .then_inc(dve_step, t.dve_step.inc())
                dve.wait_ge(dve_step, t.dve_step.now())
                for r in range(ROUNDS):
                    last = V.tensor_scalar(tops[:, r:r + 1], gate[0:1, 3:4], float(r * CAP), None, ALU.subtract)
                last.then_inc(tops_ready, t.tops_ready.inc())
                dve.wait_ge(tops_ready, t.tops_ready.now())

            V.memset(w_raw[:], 0.0).then_inc(raw_zeroed, t.raw_zeroed.inc())
            def angles(n):
                ang, turns_n = trig[:, n, :], tmp[:, 0, :]
                V.tensor_scalar(ang, trig[:, 3, :], const[:, K_FREQ + n:K_FREQ + n + 1], None, ALU.mult).then_inc(dve_step, t.dve_step.inc())
                dve.wait_ge(dve_step, t.dve_step.now())
                V.tensor_scalar(turns_n, ang, 1.0 / TWO_PI, ROUND_MAGIC, ALU.mult, ALU.add).then_inc(dve_step, t.dve_step.inc())
                dve.wait_ge(dve_step, t.dve_step.now())
                V.tensor_scalar(turns_n, turns_n, ROUND_MAGIC, None, ALU.subtract).then_inc(dve_step, t.dve_step.inc())
                dve.wait_ge(dve_step, t.dve_step.now())
                for part in (PI_A, PI_B, PI_C):
                    V.scalar_tensor_tensor(out=ang, in0=turns_n, scalar=-part, in1=ang, op0=ALU.mult, op1=ALU.add).then_inc(dve_step, t.dve_step.inc())
                    dve.wait_ge(dve_step, t.dve_step.now())
                V.tensor_scalar(ang, ang, SIN_MAX, -SIN_MAX, ALU.min, ALU.max).then_inc(ang_ready, t.ang_ready.inc())

            dve.wait_ge(table_landed, 32)
            V.tensor_copy(trig[:, 3, :], pos_i[:]).then_inc(dve_step, t.dve_step.inc())
            dve.wait_ge(dve_step, t.dve_step.now())
            angles(0)
            clear_sum()
            for k in range(KC):
                dve.wait_ge(x_turns, t.x_turns.next())
                V.tensor_copy(x[:, k, :], ps[:, k % 2, :]).then_inc(x_turned, t.x_turned.inc())
                if k >= 2:
                    add_square(k % 2)
            for s in range(2):
                add_square(s)
            dve.wait_ge(setup_landed, SETUP_LANDED)
            dve.wait_ge(x_turned, t.x_turned.now())

            for l in range(DEPTH):
                norm(x, KC, gains[:, 3 * l, :], h_hi, h_lo)
                V.memset(q_all[HD:HD + 1, :, :], 1.0).then_inc(qrow_ready, t.qrow_ready.inc())
                with turns(dve, 3, {t.unit_done: 2, t.q_ready: 1}) as j:
                    dve.wait_ge(unit_done, t.unit_done.next())
                    V.tensor_scalar(q_all[0:HD, j * 2, :], ps[0:HD, 0, :], HD**-0.5, None, ALU.mult)
                    V.tensor_scalar(q_all[0:HD, j * 2 + 1, :], ps[HD:P, 0, :], HD**-0.5, None, ALU.mult).then_inc(q_ready, t.q_ready.inc())
                    t.unit_done.add()
                if l == 0:
                    angles(1)
                dve.wait_ge(unit_done, t.unit_done.next())
                V.tensor_scalar(scan_t[:, 0, :], ps[0:FOX_HEADS, 5, :], b_forget[:, l:l + 1], None, ALU.add).then_inc(fz_taken, t.fz_taken.inc())
                dve.wait_ge(fz_taken, t.fz_taken.now())
                V.tensor_scalar(scan[:, 1, :], scan_t[:, 0, :], 0.0, None, ALU.min).then_inc(dve_step, t.dve_step.inc())
                dve.wait_ge(dve_step, t.dve_step.now())
                dve.wait_ge(fz_ready, t.fz_ready.next())
                V.tensor_tensor(scan[:, 0, :], scan_t[:, 3, :], scan[:, 1, :], ALU.subtract).then_inc(dve_step, t.dve_step.inc())
                dve.wait_ge(dve_step, t.dve_step.now())
                d, at_row = 1, 0
                while d < T:
                    src, dst = scan[:, at_row, :], scan[:, 1 - at_row, :]
                    V.tensor_copy(dst[:, 0:d], src[:, 0:d]).then_inc(dve_step, t.dve_step.inc())
                    dve.wait_ge(dve_step, t.dve_step.now())
                    add = V.tensor_tensor(dst[:, d:T], src[:, d:T], src[:, 0:T - d], ALU.add)
                    d, at_row = 2 * d, 1 - at_row
                    if d < T:
                        add.then_inc(dve_step, t.dve_step.inc())
                        dve.wait_ge(dve_step, t.dve_step.now())
                    else:
                        add.then_inc(negd_ready, t.negd_ready.inc())
                assert at_row == 1
                v_blocks(3)
                attention(3, 0, 0)
                if l == 0:
                    dve.wait_ge(act_step, t.act_step.now() + 4)
                    t.act_step.add(4)
                V.memset(k_all[HD:HD + 1, :, :], 0.0).then_inc(qrow_ready, t.qrow_ready.inc())
                with turns(dve, 3, {t.unit_done: 2, t.raw_ready: 2, t.rot_done: 2, t.dve_step: 2, t.rope_ready: 2}) as j:
                    for s, dst in enumerate((q_all, k_all)):
                        t.unit_done.add()
                        rope(s, 2 + s, P, cos_d, sin_d, [(dst[0:HD, j * 2, :], 0, HD), (dst[0:HD, j * 2 + 1, :], HD, P)])
                v_blocks(3)
                attention(3, 3, 1)
                t.unit_done.add(5), t.sq_ready.add(4)
                norm(cq_raw, 2, gains_r[:, 2 * l, :], cn_hi, cn_lo)
                dve.wait_ge(hlo_ready, t.hlo_ready.now())
                rope(0, 5, QK_M, cos_m, sin_m, [(k_all[NOPE:QK_M, hd, :], NOPE, QK_M) for hd in range(MLA_HEADS)])
                inverse_root()
                t.unit_done.add()
                for hd in range(MLA_HEADS):
                    rope(hd % 2, 5 + hd % 2, QK_M, cos_m, sin_m, [(q_all[0:QK_M, hd, :], 0, QK_M)])
                dve.wait_ge(rope_ready, t.rope_ready.now())
                norm(ckv_raw, 2, gains_r[:, 2 * l + 1, :], cn_hi, cn_lo, inverted=True)
                t.unit_done.add()
                for hd in range(MLA_HEADS):
                    t.raw_ready.add()
                    dve.wait_ge(v_turns, t.v_turns.next())
                    V.tensor_copy(v_all[:, :, hd * HD:(hd + 1) * HD],
                                         ps[:, 4 + hd % 2, :].rearrange("p (b n) -> p b n", b=TB)[:, :, NOPE:P]).then_inc(v_ready, t.v_ready.inc())
                attention(2, 6, 0)
                with turns(dve, KC, {t.unit_done: 4, t.sig_ready: 3, t.dve_step: 2, t.m_ready: 1, t.mhi_ready: 1, t.mlo_ready: 1}) as m:
                    dve.wait_ge(unit_done, t.unit_done.next(4))
                    dve.wait_ge(sig_ready, t.sig_ready.next(3))
                    for b in range(3):
                        last = V.tensor_tensor(tmp[:, b, :], sg[:, b, :], ps[:, 3 + b, :], ALU.mult)
                    last.then_inc(dve_step, t.dve_step.inc())
                    dve.wait_ge(dve_step, t.dve_step.now())
                    V.tensor_tensor(tmp[:, 0, :], tmp[:, 0, :], tmp[:, 1, :], ALU.add).then_inc(dve_step, t.dve_step.inc())
                    dve.wait_ge(dve_step, t.dve_step.now())
                    V.tensor_tensor(tmp[:, 0, :], tmp[:, 0, :], tmp[:, 2, :], ALU.add).then_inc(m_ready, t.m_ready.inc())
                    dve.wait_ge(mhi_ready, t.mhi_ready.next())
                    dve.wait_ge(m_ready, t.m_ready.now())
                    V.tensor_tensor(m_lo[:, m, :], tmp[:, 0, :], m_hi[:, m, :].bitcast(F32), ALU.subtract).then_inc(mlo_ready, t.mlo_ready.inc())
                clear_sum()
                with turns(dve, KC // 2, {t.unit_done: 2, t.x_upd: 2, t.sq_ready: 2, t.sum_ready: 2}) as m:
                    for s in range(2):
                        dve.wait_ge(unit_done, t.unit_done.next())
                        V.tensor_tensor(x[:, m * 2 + s, :], x[:, m * 2 + s, :], ps[:, 6 + s, :], ALU.add).then_inc(x_upd, t.x_upd.inc())
                        add_square(s)
                dve.wait_ge(x_upd, t.x_upd.now())
                norm(x, KC, gains[:, 3 * l + 1, :], h_hi, h_lo)
                for c in range(PLE // P):
                    dve.wait_ge(phi_ready, t.phi_ready.next())
                    V.tensor_tensor(p_lo[:, c, :], ps[:, 4 + c, :], p_hi[:, c, :].bitcast(F32), ALU.subtract).then_inc(plo_ready, t.plo_ready.inc())

                def expert(half):
                    with turns(dve, FB, {t.unit_done: 2, t.sig_ready: 1, t.af_ready: 1, t.ahi_ready: 1, t.alo_ready: 1}) as f:
                        dve.wait_ge(unit_done, t.unit_done.next(2))
                        dve.wait_ge(sig_ready, t.sig_ready.next())
                        V.tensor_tensor(tmp[:, 0, :], sg[:, 0, :], ps[:, 1, :], ALU.mult).then_inc(af_ready, t.af_ready.inc())
                        dve.wait_ge(ahi_ready, t.ahi_ready.next())
                        dve.wait_ge(af_ready, t.af_ready.now())
                        V.tensor_tensor(a_lo[:, f, :], tmp[:, 0, :], a_hi[:, f, :].bitcast(F32), ALU.subtract).then_inc(alo_ready, t.alo_ready.inc())
                    if half:
                        clear_sum()
                    with turns(dve, KC // 2, {t.unit_done: 2, t.x_upd: 2} | ({t.sq_ready: 2, t.sum_ready: 2} if half else {})) as m:
                        for s in range(2):
                            dve.wait_ge(unit_done, t.unit_done.next())
                            V.tensor_tensor(x[:, m * 2 + s, :], x[:, m * 2 + s, :], ps[:, 2 + s, :], ALU.add).then_inc(x_upd, t.x_upd.inc())
                            if half:
                                add_square(s)
                    dve.wait_ge(x_upd, t.x_upd.now())

                def select(e):
                    V.tensor_copy(comb_e[:], comb_tab[:, :, bass.ds(e, 1)])
                    V.tensor_copy(rank_e[:], rank_tab[:, :, bass.ds(e, 1)]).then_inc(moe_step, t.moe_step.inc())
                    dve.wait_ge(moe_step, t.moe_step.now())
                    for b in range(TB):
                        last = V.tensor_scalar(sel[:, b, :], const[:, K_SLOTS:K_SLOTS + CAP], rank_e[:, b, :], None, ALU.is_equal)
                    last.then_inc(sel_ready, t.sel_ready.inc())

                def up_block(f, n):
                    dve.wait_ge(expert_unit_done, t.expert_unit_done.next(2))
                    dve.wait_ge(silu_ready, t.silu_ready.next())
                    V.tensor_tensor(ga[:, f, :], silu[:, n, :], ps[:, 2 * n + 1, 0:CAP], ALU.mult)\
                        .then_inc(expert_act_ready, t.expert_act_ready.inc())

                def take_down(m):
                    dve.wait_ge(expert_unit_done, t.expert_unit_done.next())
                    V.tensor_copy(y_t[:, m, :], ps[:, (2 * FB + m) % RING, 0:CAP]).then_inc(y_taken, t.y_taken.inc())

                def weigh(half):
                    for tile in range(2):
                        dve.wait_ge(y_turned, t.y_turned.next())
                        V.tensor_scalar(tmp[:, 2 * half + tile, :], ps[:, 6 + tile, :], slot_w[:, tile:tile + 1], None, ALU.mult)\
                            .then_inc(y32_ready, t.y32_ready.inc())

                def lower_outputs(half):
                    dve.wait_ge(y32_ready, t.y32_ready.now())
                    for tile in range(2):
                        dve.wait_ge(yhi_ready, t.yhi_ready.next())
                        part = (slice(None), tile, slice(half * T, (half + 1) * T))
                        V.tensor_tensor(y_lo[part], tmp[:, 2 * half + tile, :], y_hi[part].bitcast(F32), ALU.subtract)\
                            .then_inc(ylo_ready, t.ylo_ready.inc())

                def gathered_expert(e):
                    for pair in range(1, KC // 2, 2):
                        t.gathered.add()
                        dve.wait_ge(gathered, t.gathered.next())
                        V.tensor_copy(hg[:, 2 * pair:2 * pair + 2, :], ps[:, 7, 0:2 * CAP].rearrange("p (k n) -> p k n", k=2))\
                            .then_inc(hgodd_ready, t.hgodd_ready.inc())
                    dve.wait_ge(cw_done, t.cw_done.next())
                    V.tensor_copy(slot_w[:], ps[:, 6, 0:2]).then_inc(cw_ready, t.cw_ready.inc())
                    select(e + 1)
                    with turns(dve, FB // 3, {t.expert_unit_done: RING, t.silu_ready: 3, t.expert_act_ready: 3}) as f:
                        for n in range(3):
                            up_block(f * 3 + n, n)
                    for n in range(FB % 3):
                        up_block(FB - FB % 3 + n, n)
                    for m in range(KC - 2):
                        take_down(m)
                    dve.wait_ge(cw_ready, t.cw_ready.now())
                    weigh(0)
                    take_down(KC - 2)
                    lower_outputs(0)
                    take_down(KC - 1)
                    weigh(1)
                    lower_outputs(1)
                    for k in range(KC):
                        dve.wait_ge(scattered, t.scattered.next())
                        V.tensor_tensor(x[:, k, :], x[:, k, :], ps[:, k % 4, :], ALU.add).then_inc(tokens_added, t.tokens_added.inc())
                    dve.wait_ge(tokens_added, t.tokens_added.now())
                    dve.wait_ge(ylo_ready, t.ylo_ready.now())

                if l % 2 == 0:
                    for half in range(2):
                        expert(half)
                else:
                    V.memset(comb_tab[:], 0.0)
                    V.memset(rank_tab[:], -1.0).then_inc(moe_step, t.moe_step.inc())
                    dve.wait_ge(moe_step, t.moe_step.now())
                    dve.wait_ge(unit_done, t.unit_done.next())
                    routing()
                    per_expert = {t.sel_ready: 1, t.moe_step: 1, t.gathered: KC // 2, t.hgodd_ready: 2, t.cw_done: 1, t.cw_ready: 1,
                                  t.expert_unit_done: EXPERT_UNITS, t.silu_ready: FB, t.expert_act_ready: FB, t.y_taken: KC,
                                  t.y_turned: 4, t.y32_ready: 4, t.yhi_ready: 4, t.ylo_ready: 4, t.scattered: KC,
                                  t.tokens_added: KC}
                    with turns(dve, ROUNDS, {c: EXPERTS * n for c, n in per_expert.items()}
                               | {t.sel_ready: EXPERTS + 1, t.moe_step: EXPERTS + 2}) as r:
                        with dve.If(dve.value_load(tops[0:1, bass.ds(r, 1)]) > 0):
                            select(0)
                            with turns(dve, EXPERTS, per_expert) as e:
                                gathered_expert(e)
                            V.tensor_scalar(rank_tab[:], rank_tab[:], float(CAP), None, ALU.subtract).then_inc(moe_step, t.moe_step.inc())
                            dve.wait_ge(moe_step, t.moe_step.now())
                            V.memset(gate[:, 1:2], 0.0)
                    V.memset(gate[:, 2:3], 0.0).then_inc(moe_done, t.moe_done.inc())
                    clear_sum()
                    for k in range(KC):
                        add_square(k % 2)
                t.unit_done.add(2)
                norm(x, KC, gains[:, 3 * l + 2, :], h_hi, h_lo)
                dve.wait_ge(pp_ready, t.pp_ready.next(KC))
                clear_sum()
                with turns(dve, KC // 2, {t.unit_done: 2, t.sig_ready: 2, t.dve_step: 2, t.x_upd: 2, t.sq_ready: 2, t.sum_ready: 2}) as m:
                    for s in range(2):
                        t.unit_done.add()
                        dve.wait_ge(sig_ready, t.sig_ready.next())
                        V.tensor_tensor(tmp[:, s, :], sg[:, s, :], pp[:, m * 2 + s, :], ALU.mult).then_inc(dve_step, t.dve_step.inc())
                        dve.wait_ge(dve_step, t.dve_step.now())
                        V.tensor_tensor(x[:, m * 2 + s, :], x[:, m * 2 + s, :], tmp[:, s, :], ALU.add).then_inc(x_upd, t.x_upd.inc())
                        add_square(s)
                dve.wait_ge(x_upd, t.x_upd.now())
            dve.wait_ge(root_ready, t.root_ready.next())
            V.reciprocal(rstd[:], rstd[:]).then_inc(dve_step, t.dve_step.inc())
            dve.wait_ge(dve_step, t.dve_step.now())
            for k in range(KC):
                V.scalar_tensor_tensor(out=x[:, k, :], in0=x[:, k, :], scalar=gains[:, 3 * DEPTH, k:k + 1],
                                              in1=rstd[:], op0=ALU.mult, op1=ALU.mult).then_inc(xn_ready, t.xn_ready.inc())


_INS = ["x", "p", "positions", "mix_norm", "w_in", "b_forget", "mla_q_norm", "mla_kv_norm", "w_uq", "w_ukv",
        "w_br_fox", "w_br_dil", "w_br_mla", "w_out", "ffn_norm", "w_ffn_gate", "w_ffn_up", "w_ffn_down",
        "w_router", "w_exp_gate", "w_exp_up", "w_exp_down", "ple_norm", "w_ple_gate", "w_ple_proj", "final_norm"]


def kernel(**inputs):
    import numpy as _np
    import concourse.bacc as _bacc
    from concourse import mybir as _mybir
    from concourse.bass_utils import run_bass_kernel_spmd as _run

    nc = _bacc.Bacc("TRN2", target_bir_lowering=False, num_devices=1)
    arrays, aps = {}, {}
    tables = {"const": constant_table()}
    for name in _INS + ["const"]:
        array = _np.ascontiguousarray(tables[name] if name in tables else inputs[name])
        arrays[f"in_{name}_dram"] = array
        aps[name] = nc.dram_tensor(f"in_{name}_dram", array.shape, _mybir.dt.from_np(array.dtype), kind="ExternalInput").ap()
    out = nc.dram_tensor("out_0_dram", (1, T, D), _mybir.dt.float32, kind="ExternalOutput").ap()
    build_trunk(nc, aps, out)
    r = _run(nc, [arrays], core_ids=[0])
    return r.results[0]["out_0_dram"]
```
